# Optimizing a Trainium2 kernel written in Bass

```python
import math
import jax
import jax.numpy as jnp
from jax import lax
import numpy as np

D_MODEL = 1024
BATCH = 1
SEQ = 256
DEPTH = 2

CHUNK = 64
Q_BLOCK = 128
NORM_EPS = 1e-6

DA_HEADS = 4
DA_HEAD_DIM = 64
DA_V_DIM = 2 * DA_HEAD_DIM
DA_WIDTH = DA_HEADS * DA_V_DIM
ROT_DIM = DA_HEAD_DIM // 4
ROPE_THETA = 500000.0

SSM_GROUP = 16
SSM_GROUPS = 16
SSM_WIDTH = SSM_GROUP * SSM_GROUPS
SSM_STATE = 64

RW_HEADS = 4
RW_HEAD_DIM = 64
RW_WIDTH = RW_HEADS * RW_HEAD_DIM
RW_DECAY_RANK = 32
RW_AAA_RANK = 32
RW_GATE_RANK = 64
RW_LN_EPS = 64e-5

MIX_WIDTH = DA_WIDTH + SSM_WIDTH + RW_WIDTH
DA_COLS = 3 * DA_WIDTH
RW_COLS = 3 * RW_WIDTH + RW_DECAY_RANK + RW_AAA_RANK + RW_GATE_RANK
IN_COLS = DA_COLS + SSM_WIDTH + RW_COLS

PEER_HEADS = 8
N_KEYS = 128
N_EXPERTS = N_KEYS * N_KEYS
PEER_KEY_DIM = 128
PEER_TOPK = 16
PEER_TOKEN_BLOCK = 128

kernel_name = 'hybrid_diffattn_s5_rwkv7_peer'

def rms_norm(x, g, eps=NORM_EPS):
    xf = x.astype(jnp.float32)
    y = xf * lax.rsqrt(jnp.mean(xf * xf, axis=-1, keepdims=True) + eps)
    return (y * g.astype(jnp.float32)).astype(x.dtype)

def partial_rope(t, cos, sin):
    half = ROT_DIM // 2
    c = cos[:, :, None, None, :].astype(t.dtype)
    s = sin[:, :, None, None, :].astype(t.dtype)
    r1, r2, rest = t[..., :half], t[..., half:ROT_DIM], t[..., ROT_DIM:]
    return jnp.concatenate([r1 * c - r2 * s, r2 * c + r1 * s, rest], axis=-1)

def diff_attention(cols, cos, sin, q_norm, k_norm, lam, subln, layer):
    bsz, seq, _ = cols.shape
    dt = cols.dtype
    q = cols[..., :DA_WIDTH].reshape(bsz, seq, DA_HEADS, 2, DA_HEAD_DIM)
    k = cols[..., DA_WIDTH:2 * DA_WIDTH].reshape(bsz, seq, DA_HEADS, 2, DA_HEAD_DIM)
    v = cols[..., 2 * DA_WIDTH:].reshape(bsz, seq, DA_HEADS, DA_V_DIM)
    q = partial_rope(rms_norm(q, q_norm), cos, sin)
    k = partial_rope(rms_norm(k, k_norm), cos, sin)
    lam_init = 0.8 - 0.6 * math.exp(-0.3 * layer)
    lf = lam.astype(jnp.float32)
    lam_full = jnp.exp(jnp.sum(lf[0] * lf[1])) - jnp.exp(jnp.sum(lf[2] * lf[3])) + lam_init
    scale = DA_HEAD_DIM ** -0.5
    outs = []
    for blk in range(seq // Q_BLOCK):
        q0 = blk * Q_BLOCK
        kv_end = q0 + Q_BLOCK
        s = jnp.einsum('bqhmd,bkhmd->bhmqk', q[:, q0:kv_end], k[:, :kv_end]).astype(jnp.float32) * scale
        q_chunk = (q0 + jnp.arange(Q_BLOCK)) // CHUNK
        k_chunk = jnp.arange(kv_end) // CHUNK
        s = jnp.where(k_chunk[None, :] <= q_chunk[:, None], s, -jnp.inf)
        p = jax.nn.softmax(s, axis=-1)
        a = p[:, :, 0] - lam_full * p[:, :, 1]
        outs.append(jnp.einsum('bhqk,bkhe->bqhe', a.astype(dt), v[:, :kv_end]))
    o = jnp.concatenate(outs, axis=1)
    o = rms_norm(o, subln) * (1.0 - lam_init)
    return o.reshape(bsz, seq, DA_WIDTH)

def _complex_affine_combine(e1, e2):
    a1r, a1i, b1r, b1i = e1
    a2r, a2i, b2r, b2i = e2
    ar = a2r * a1r - a2i * a1i
    ai = a2r * a1i + a2i * a1r
    br = a2r * b1r - a2i * b1i + b2r
    bi = a2r * b1i + a2i * b1r + b2i
    return (ar, ai, br, bi)

def s5_mixer(u, lam_re, lam_im, b_re, b_im, c_re, c_im, d_skip, log_dt, w_glu, b_glu, out_norm):
    bsz, seq, _ = u.shape
    f32 = jnp.float32
    uf = u.astype(f32).reshape(bsz, seq, SSM_GROUPS, SSM_GROUP)
    lr = jnp.minimum(lam_re.astype(f32), -1e-4)
    li = lam_im.astype(f32)
    step = jnp.exp(log_dt.astype(f32))[:, None]
    mag = jnp.exp(lr * step)
    abar_re = mag * jnp.cos(li * step)
    abar_im = mag * jnp.sin(li * step)
    den = lr * lr + li * li
    coef_re = ((abar_re - 1.0) * lr + abar_im * li) / den
    coef_im = (abar_im * lr - (abar_re - 1.0) * li) / den
    br, bi = b_re.astype(f32), b_im.astype(f32)
    bbar_re = coef_re[..., None] * br - coef_im[..., None] * bi
    bbar_im = coef_re[..., None] * bi + coef_im[..., None] * br
    bu_re = jnp.einsum('blgh,gph->lbgp', uf, bbar_re)
    bu_im = jnp.einsum('blgh,gph->lbgp', uf, bbar_im)
    a_re = jnp.broadcast_to(abar_re[None, None], (seq, 1, SSM_GROUPS, SSM_STATE))
    a_im = jnp.broadcast_to(abar_im[None, None], (seq, 1, SSM_GROUPS, SSM_STATE))
    _, _, xr, xi = lax.associative_scan(_complex_affine_combine, (a_re, a_im, bu_re, bu_im), axis=0)
    y = (jnp.einsum('lbgp,ghp->blgh', xr, c_re.astype(f32))
         - jnp.einsum('lbgp,ghp->blgh', xi, c_im.astype(f32))
         + d_skip.astype(f32) * uf)
    yg = jax.nn.gelu(y.reshape(bsz, seq, SSM_WIDTH), approximate=False)
    out = yg * jax.nn.sigmoid(yg @ w_glu.astype(f32) + b_glu.astype(f32))
    return rms_norm(out, out_norm).astype(u.dtype)

def rwkv7_mixer(cols, mu, decay_up, decay_w0, aaa_up, aaa_a0, gate_up, k_k, k_a, r_k, ln_w, ln_b):
    bsz, seq, _ = cols.shape
    f32 = jnp.float32
    c = cols.astype(f32)
    prev = jnp.pad(c, ((0, 0), (1, 0), (0, 0)))[:, :-1]
    c = c + (prev - c) * mu.astype(f32)
    o1, o2, o3 = RW_WIDTH, 2 * RW_WIDTH, 3 * RW_WIDTH
    o4, o5 = o3 + RW_DECAY_RANK, o3 + RW_DECAY_RANK + RW_AAA_RANK
    r, k, v = c[..., :o1], c[..., o1:o2], c[..., o2:o3]
    wd, ad, gd = c[..., o3:o4], c[..., o4:o5], c[..., o5:]
    w_log = -jax.nn.softplus(-(decay_w0.astype(f32) + jnp.tanh(wd) @ decay_up.astype(f32))) - 0.5
    decay = jnp.exp(-jnp.exp(w_log))
    a = jax.nn.sigmoid(aaa_a0.astype(f32) + ad @ aaa_up.astype(f32))
    g = jax.nn.sigmoid(gd) @ gate_up.astype(f32)
    heads = lambda t: t.reshape(bsz, seq, RW_HEADS, RW_HEAD_DIM)
    kk = heads(k * k_k.astype(f32))
    kk = kk / jnp.maximum(jnp.sqrt(jnp.sum(kk * kk, axis=-1, keepdims=True)), 1e-12)
    k = k * (1.0 + (a - 1.0) * k_a.astype(f32))
    r, k, v, decay, a = heads(r), heads(k), heads(v), heads(decay), heads(a)
    bvec = kk * a

    def step(S, inp):
        r_t, w_t, k_t, v_t, kk_t, b_t = inp
        sa = jnp.einsum('bhij,bhj->bhi', S, -kk_t)
        S = S * w_t[:, :, None, :] + sa[..., None] * b_t[:, :, None, :] + v_t[..., None] * k_t[:, :, None, :]
        return S, jnp.einsum('bhij,bhj->bhi', S, r_t)

    xs = tuple(jnp.moveaxis(t, 1, 0) for t in (r, decay, k, v, kk, bvec))
    S0 = jnp.zeros((bsz, RW_HEADS, RW_HEAD_DIM, RW_HEAD_DIM), f32)
    _, y = lax.scan(step, S0, xs)
    y = jnp.moveaxis(y, 0, 1)
    mean = jnp.mean(y, axis=-1, keepdims=True)
    var = jnp.mean(jnp.square(y - mean), axis=-1, keepdims=True)
    y = ((y - mean) * lax.rsqrt(var + RW_LN_EPS)).reshape(bsz, seq, RW_WIDTH)
    y = y * ln_w.astype(f32) + ln_b.astype(f32)
    bonus = jnp.sum(r * k * r_k.astype(f32), axis=-1, keepdims=True) * v
    y = y + bonus.reshape(bsz, seq, RW_WIDTH)
    return (y * g).astype(cols.dtype)

def peer_ffn(h, w_q, sub_keys, u_tab, v_tab):
    bsz, seq, dm = h.shape
    blocks = h.reshape(bsz * seq // PEER_TOKEN_BLOCK, PEER_TOKEN_BLOCK, dm)

    def block_fn(hb):
        q = (hb @ w_q).reshape(PEER_TOKEN_BLOCK, PEER_HEADS, 2, PEER_KEY_DIM)
        s = jnp.einsum('thmd,hmkd->thmk', q, sub_keys).astype(jnp.float32)
        top_s, top_i = lax.top_k(s, PEER_TOPK)
        cand_s = top_s[:, :, 0, :, None] + top_s[:, :, 1, None, :]
        cand_i = top_i[:, :, 0, :, None] * N_KEYS + top_i[:, :, 1, None, :]
        cand_s = cand_s.reshape(PEER_TOKEN_BLOCK, PEER_HEADS, PEER_TOPK * PEER_TOPK)
        cand_i = cand_i.reshape(PEER_TOKEN_BLOCK, PEER_HEADS, PEER_TOPK * PEER_TOPK)
        best_s, best_pos = lax.top_k(cand_s, PEER_TOPK)
        expert = jnp.take_along_axis(cand_i, best_pos, axis=-1)
        gate = jax.nn.softmax(best_s, axis=-1)
        u_sel = jnp.take(u_tab, expert, axis=0)
        act = jax.nn.gelu(jnp.einsum('thkd,td->thk', u_sel, hb).astype(jnp.float32), approximate=False)
        v_sel = jnp.take(v_tab, expert, axis=0)
        return jnp.einsum('thk,thkd->td', (gate * act).astype(hb.dtype), v_sel)

    return lax.map(block_fn, blocks).reshape(bsz, seq, dm)

def setup_inputs(seed: int = 0) -> dict:
    key = jax.random.key(seed)
    keys = list(jax.random.split(key, 48))
    f32 = jnp.float32

    def nxt():
        return keys.pop()

    def nrm(shape, scale):
        return jax.random.normal(nxt(), shape, f32) * scale

    def gain(shape):
        return 1.0 + nrm(shape, 0.02)

    x = nrm((BATCH, SEQ, D_MODEL), 1.0)
    offs = jax.random.randint(nxt(), (BATCH, 1), 0, 64, dtype=jnp.int32) * CHUNK
    positions = (offs + jnp.arange(SEQ, dtype=jnp.int32)[None, :]).astype(jnp.int32)
    n_idx = jnp.arange(SSM_STATE, dtype=f32)
    decay_base = jnp.tile(jnp.linspace(-6.0, -1.0, RW_HEAD_DIM, dtype=f32), RW_HEADS)
    return {
        'x': x,
        'positions': positions,
        'norm_mix': gain((DEPTH, D_MODEL)),
        'w_in': nrm((DEPTH, D_MODEL, IN_COLS), D_MODEL ** -0.5),
        'da_q_norm': gain((DEPTH, DA_HEADS, 2, DA_HEAD_DIM)),
        'da_k_norm': gain((DEPTH, DA_HEADS, 2, DA_HEAD_DIM)),
        'da_lambda': nrm((DEPTH, 4, DA_HEAD_DIM), 0.1),
        'da_subln': gain((DEPTH, DA_V_DIM)),
        'ssm_lambda_re': -0.5 + nrm((DEPTH, SSM_GROUPS, SSM_STATE), 0.01),
        'ssm_lambda_im': math.pi * n_idx + nrm((DEPTH, SSM_GROUPS, SSM_STATE), 0.01),
        'ssm_b_re': nrm((DEPTH, SSM_GROUPS, SSM_STATE, SSM_GROUP), (2 * SSM_GROUP) ** -0.5),
        'ssm_b_im': nrm((DEPTH, SSM_GROUPS, SSM_STATE, SSM_GROUP), (2 * SSM_GROUP) ** -0.5),
        'ssm_c_re': nrm((DEPTH, SSM_GROUPS, SSM_GROUP, SSM_STATE), (2 * SSM_STATE) ** -0.5),
        'ssm_c_im': nrm((DEPTH, SSM_GROUPS, SSM_GROUP, SSM_STATE), (2 * SSM_STATE) ** -0.5),
        'ssm_d': nrm((DEPTH, SSM_GROUPS, SSM_GROUP), 1.0),
        'ssm_log_dt': jax.random.uniform(nxt(), (DEPTH, SSM_GROUPS), f32, math.log(1e-3), math.log(1e-1)),
        'ssm_w_glu': nrm((DEPTH, SSM_WIDTH, SSM_WIDTH), SSM_WIDTH ** -0.5),
        'ssm_b_glu': nrm((DEPTH, SSM_WIDTH), 0.02),
        'ssm_out_norm': gain((DEPTH, SSM_WIDTH)),
        'rw_mu': jax.random.uniform(nxt(), (DEPTH, RW_COLS), f32, 0.0, 1.0),
        'rw_decay_up': nrm((DEPTH, RW_DECAY_RANK, RW_WIDTH), 0.1),
        'rw_decay_w0': decay_base + nrm((DEPTH, RW_WIDTH), 0.1),
        'rw_aaa_up': nrm((DEPTH, RW_AAA_RANK, RW_WIDTH), 0.1),
        'rw_aaa_a0': nrm((DEPTH, RW_WIDTH), 0.1),
        'rw_gate_up': nrm((DEPTH, RW_GATE_RANK, RW_WIDTH), RW_GATE_RANK ** -0.5),
        'rw_k_k': 0.85 + nrm((DEPTH, RW_WIDTH), 0.02),
        'rw_k_a': gain((DEPTH, RW_WIDTH)),
        'rw_r_k': nrm((DEPTH, RW_HEADS, RW_HEAD_DIM), 0.1),
        'rw_ln_w': gain((DEPTH, RW_WIDTH)),
        'rw_ln_b': nrm((DEPTH, RW_WIDTH), 0.02),
        'w_out': nrm((DEPTH, MIX_WIDTH, D_MODEL), MIX_WIDTH ** -0.5),
        'norm_ffn': gain((DEPTH, D_MODEL)),
        'peer_w_q': nrm((DEPTH, D_MODEL, PEER_HEADS * 2 * PEER_KEY_DIM), D_MODEL ** -0.5),
        'peer_sub_keys': nrm((DEPTH, PEER_HEADS, 2, N_KEYS, PEER_KEY_DIM), PEER_KEY_DIM ** -0.5),
        'peer_u': nrm((DEPTH, N_EXPERTS, D_MODEL), D_MODEL ** -0.5),
        'peer_v': nrm((DEPTH, N_EXPERTS, D_MODEL), PEER_TOPK ** -0.5),
    }

def reference(x, positions, norm_mix, w_in, da_q_norm, da_k_norm, da_lambda, da_subln,
              ssm_lambda_re, ssm_lambda_im, ssm_b_re, ssm_b_im, ssm_c_re, ssm_c_im, ssm_d,
              ssm_log_dt, ssm_w_glu, ssm_b_glu, ssm_out_norm, rw_mu, rw_decay_up, rw_decay_w0,
              rw_aaa_up, rw_aaa_a0, rw_gate_up, rw_k_k, rw_k_a, rw_r_k, rw_ln_w, rw_ln_b,
              w_out, norm_ffn, peer_w_q, peer_sub_keys, peer_u, peer_v):
    inv_freq = ROPE_THETA ** (-jnp.arange(0, ROT_DIM, 2, dtype=jnp.float32) / ROT_DIM)
    ang = positions.astype(jnp.float32)[..., None] * inv_freq
    cos, sin = jnp.cos(ang), jnp.sin(ang)
    for l in range(DEPTH):
        h = rms_norm(x, norm_mix[l])
        cols = h @ w_in[l]
        cols_a = cols[..., :DA_COLS]
        cols_b = cols[..., DA_COLS:DA_COLS + SSM_WIDTH]
        cols_c = cols[..., DA_COLS + SSM_WIDTH:]
        y_a = diff_attention(cols_a, cos, sin, da_q_norm[l], da_k_norm[l], da_lambda[l], da_subln[l], l)
        y_b = s5_mixer(cols_b, ssm_lambda_re[l], ssm_lambda_im[l], ssm_b_re[l], ssm_b_im[l],
                       ssm_c_re[l], ssm_c_im[l], ssm_d[l], ssm_log_dt[l], ssm_w_glu[l],
                       ssm_b_glu[l], ssm_out_norm[l])
        y_c = rwkv7_mixer(cols_c, rw_mu[l], rw_decay_up[l], rw_decay_w0[l], rw_aaa_up[l],
                          rw_aaa_a0[l], rw_gate_up[l], rw_k_k[l], rw_k_a[l], rw_r_k[l],
                          rw_ln_w[l], rw_ln_b[l])
        mixed = jnp.concatenate([y_a.astype(x.dtype), y_b.astype(x.dtype), y_c.astype(x.dtype)], axis=-1)
        x = x + mixed @ w_out[l]
        x = x + peer_ffn(rms_norm(x, norm_ffn[l]), peer_w_q[l], peer_sub_keys[l], peer_u[l], peer_v[l])
    return x


_drawn_inputs = setup_inputs


def setup_inputs(seed=0):
    import zlib

    import numpy as np

    out = dict(_drawn_inputs(seed))
    spreads = {}
    factors = {'da_q_norm': 3.265,
     'da_k_norm': 3.141,
     'ssm_lambda_re': 8.0,
     'ssm_b_glu': 4.935,
     'ssm_out_norm': 3.234,
     'rw_decay_up': 3.299,
     'rw_aaa_a0': 3.017,
     'rw_k_k': 4.624,
     'rw_k_a': 4.047,
     'rw_ln_w': 4.679,
     'rw_ln_b': 4.597,
     'norm_ffn': 2.767}
    for name, (base, spread) in spreads.items():
        noise = np.random.default_rng([zlib.crc32(name.encode()), seed]).standard_normal(out[name].shape)
        drawn = base * np.exp(spread * noise) if base else spread * noise
        out[name] = jnp.asarray(drawn.astype(out[name].dtype))
    for name, factor in factors.items():
        out[name] = (out[name] * factor).astype(out[name].dtype)
    return out
```

```python
import math
from contextlib import ExitStack

import numpy as np

import concourse.bass as bass
from concourse import mybir

F32 = mybir.dt.float32
I32 = mybir.dt.int32
U32 = mybir.dt.uint32
ALU = mybir.AluOpType
ACT = mybir.ActivationFunctionType
AX = mybir.AxisListType

P = 128
D_MODEL = 1024
SEQ = 256
DEPTH = 2
TILES = SEQ // P
UNITS = DEPTH * TILES
KD = D_MODEL // P
CHUNK = 64
NORM_EPS = 1e-6
RW_EPS = 64e-5
HEADS = 4
HD = 64
DA_COLS = 1536
BLOCKS = 9
GROUPS, STATE, GCH = 16, 64, 16
SB = GROUPS * STATE // P
PEER_HEADS, NKEYS, TOPK = 8, 128, 16
HM = PEER_HEADS * 2
N_EXPERTS = NKEYS * NKEYS
SLOTS = PEER_HEADS * TOPK
RING = 8
ROUNDS = SLOTS // RING
USES = 2 * ROUNDS
CW = 256
WRING = 3
BC_CHUNKS = [(DA_COLS + CW * c, min(CW, BLOCKS * P - CW * c)) for c in range(5)]
DA_CHUNKS = [(CW * c, CW) for c in range(6)]
OUT_CHUNKS = [(CW * c, CW) for c in range(4)]
Q_CHUNKS = [(CW * c, CW) for c in range(8)]
CHUNKS = len(BC_CHUNKS) + len(DA_CHUNKS) + len(OUT_CHUNKS) + len(Q_CHUNKS)
BC_DONE, DA_DONE = (2, 4, 5), (7, 9, 11)
OUT_DONE, Q_DONE = (13, 15), (17, 19, 21, 23)
LEVELS = 7
NL = LEVELS - 1
C_DECAY = math.exp(-0.5)
SCALE = HD ** -0.5
ROT = 8
INV_FREQ = (np.float32(500000.0) ** (-np.arange(0, 16, 2, dtype=np.float32) / np.float32(16))).astype(np.float32)
TWO_PI_A = 6.28125
TWO_PI_B = float(np.float32(2 * math.pi - 6.28125))
TWO_PI_C = float(2 * math.pi - 6.28125 - TWO_PI_B)
ROUNDER = 12582912.0
PI_IN = 3.1415925
LAM_INIT = [0.8 - 0.6 * math.exp(-0.3 * layer) for layer in range(DEPTH)]

VECTORS = [("ssm_lambda_re", 8), ("ssm_lambda_im", 8), ("norm_mix", 8), ("rw_mu", 7), ("rw_decay_w0", 2),
           ("rw_aaa_a0", 2), ("ssm_b_glu", 2), ("rw_k_k", 2), ("rw_k_a", 2), ("rw_r_k", 2), ("rw_ln_w", 2),
           ("rw_ln_b", 2), ("ssm_d", 2), ("ssm_out_norm", 2), ("da_subln", 1)]
ROW = {}
_r = 0
for _name, _k in VECTORS:
    ROW[_name] = (_r, _k)
    _r += DEPTH * _k
NROWS = _r


class Chain:

    def __init__(self, sem, engine):
        self.sem, self.engine, self.count = sem, engine, 0

    def add(self, instruction):
        instruction.then_inc(self.sem, 1)
        self.count += 1

    def __call__(self, instruction):
        self.add(instruction)
        self.engine.wait_ge(self.sem, self.count)


def build_program(nc, A, out):
    ctx = ExitStack()
    with ctx:
        def sb(name, shape, dt=F32):
            return ctx.enter_context(nc.sbuf_tensor(name, shape, dt))

        def sem(name):
            return ctx.enter_context(nc.semaphore(name))

        x = sb("x", [P, TILES, D_MODEL])
        wring = sb("wring", [P, WRING, KD, CW])
        arena = sb("arena", [P, RING, D_MODEL])
        rows = [arena[:, j, :] for j in range(RING)]
        q_cm = arena[:, 0:2, :].rearrange("p a (b t) -> p (a b) t", t=P)
        scores = arena[:, 2:4, :].rearrange("p a (b t) -> p (a b) t", t=P)
        cand = arena[:, 4:6, :].rearrange("p a (b t) -> p (a b) t", t=256)
        keys_raw = arena[:, 4:6, :].rearrange("p a (b t) -> p (a b) t", t=P)
        picked = arena[:, 6:8, :].rearrange("p a (b t) -> p (a b) t", t=TOPK)
        work = sb("work", [P, 20 * 256])
        h = sb("h", [P, D_MODEL])
        h_cm = sb("h_cm", [P, KD, P])
        mixed = h_cm
        hb = sb("hb", [P, D_MODEL])
        hb_cm = sb("hb_cm", [P, KD, P])
        y_rows = sb("y_rows", [P, D_MODEL])
        keys_cm = sb("keys_cm", [P, HM, P])
        gain_ffn = sb("gain_ffn", [P, D_MODEL])
        gain_qk = sb("gain_qk", [P, 2, 512])
        prow = sb("prow", [NROWS, P])
        pcol = sb("pcol", [P, NROWS])
        half = sb("half", [P, DEPTH * 6])
        subln = sb("subln", [P, DEPTH])
        neg_lam = sb("neg_lam", [P, DEPTH])
        glu_w = sb("glu_w", [P, DEPTH, 2, 256])
        lora_w = sb("lora_w", [P, DEPTH, 256])
        bT = sb("bT", [P, DEPTH * 2, 2, P])
        cT = sb("cT", [P, DEPTH, SB, 2, 32])
        e_cos = sb("e_cos", [P, DEPTH * SB, P])
        e_sin = sb("e_sin", [P, DEPTH * SB, P])
        mag = sb("mag", [P, DEPTH * SB])
        carry = sb("carry", [P, 2, SB])
        u4 = sb("u4", [P, 4, 2, P])
        raw = sb("raw", [P, BLOCKS, P + 1])
        cc = sb("cc", [P, 7, P])
        kT = sb("kT", [P, HEADS, SEQ])
        qT = sb("qT", [P, HEADS, P])
        v_tok = sb("v_tok", [P, TILES, 512])
        cs = sb("cs", [P, 32])
        sn = sb("sn", [P, 32])
        level = sb("level", [P, LEVELS, P])
        strict = sb("strict", [P, P])
        incl = sb("incl", [P, P])
        lower0 = sb("lower0", [P, P])
        ident = sb("ident", [P, P])
        ones = sb("ones", [P, P])
        head_ones = sb("head_ones", [P, P])
        zeros = sb("zeros", [P, P])
        ramp = sb("ramp", [P, TOPK])
        small = sb("small", [P, 64])
        eps = sb("eps", [P, 2])
        cum = sb("cum", [P, 2, P + 1])
        state = sb("state", [P, 2, HD])
        state0 = sb("state0", [P, 2, HD])
        rw = {name: sb("rw_" + name, [P, 2, P]) for name in
              ("lora", "g", "kk", "a", "al", "bm", "km", "rp", "ep", "em", "eq", "k2", "rk", "y")}
        tops = sb("tops", [P, HM, TOPK])
        topi = y_rows[:, 0:256].bitcast(U32).rearrange("p (a b) -> p a b", b=TOPK)
        topf = y_rows[:, 256:512].rearrange("p (a b) -> p a b", b=TOPK)
        best = y_rows[:, 512:640].rearrange("p (a b) -> p a b", b=TOPK)
        bpos = y_rows[:, 640:768].bitcast(U32).rearrange("p (a b) -> p a b", b=TOPK)
        bhi = y_rows[:, 768:896].bitcast(U32).rearrange("p (a b) -> p a b", b=TOPK)
        fhi = sb("fhi", [P, SLOTS])
        flo = y_rows[:, 896:1024]
        expert = sb("expert", [P, SLOTS], I32)
        slot_index = sb("slot_index", [P, RING], I32)
        gate = sb("gate", [P, SLOTS])
        dots = sb("dots", [P, SLOTS])
        weight = sb("weight", [P, SLOTS])
        diag = sb("diag", [P, RING // 2, P])

        small_m = sb("small_m", [P, 64])
        small_p = sb("small_p", [P, 32])
        small_a = sb("small_a", [P, 32])
        ti_pos = sb("ti_pos", [P, TILES], I32)
        posf = sb("posf", [P, TILES])
        ang = sb("ang", [P, 2, 32])
        lrt = sb("lrt", [P, 16])
        s5p = sb("s5p", [P, 6, 16])
        c_raw = rows[0].rearrange("p (a b c) -> p a b c", a=2, b=4)
        bd = rows[1].rearrange("p (a b c) -> p a b c", a=4, b=2)
        b_raw = rows[2][:, 0:512].rearrange("p (a b c) -> p a b c", a=2, b=16)
        lam_raw = rows[2][:, 512:1024]
        lam_raw4 = lam_raw.rearrange("p (a m d) -> p a m d", m=2, d=HD)
        b_t = rows[3].rearrange("p (a b c) -> p a b c", a=4, b=16)
        ti, pi, xi = (work[:, P * i:P * i + P].bitcast(I32) for i in range(3))
        mask_i = rows[6][:, 0:LEVELS * P].bitcast(I32).rearrange("p (a b) -> p a b", b=P)
        dbl = rows[7].rearrange("p (a b) -> p a b", a=16)

        def scratch(at, shape):
            size = int(np.prod(shape))
            view = work[:, at:at + size]
            if len(shape) == 1:
                return view
            names = "abcd"[:len(shape)]
            return view.rearrange(f"p ({' '.join(names)}) -> p {' '.join(names)}",
                                  **{c: s for c, s in zip(names[1:], shape[1:])})

        mT, nT, rbT, rkT = (scratch(512 * i, [HEADS, P]) for i in range(4))
        inv, invT, prod = (scratch(2048 + 512 * i, [HEADS, P]) for i in range(3))
        ms = [scratch(3584 + 512 * i, [HEADS, P]) for i in range(2)]
        sqs = scratch(0, [2, 512])
        qk = scratch(1024, [2, 512])
        qk_tmp = scratch(2048, [4, 16, ROT])
        tok = sb("tok", [P, 3, 2, P])
        rhs = scratch(4608, [HEADS, HD])
        sa = scratch(4864, [HEADS, HD])
        zin = [scratch(1024 * i, [SB, P]) for i in range(2)]
        z = [scratch(2048 + 1024 * i, [SB, P]) for i in range(2)]
        yg = scratch(4096, [2, P])
        glu_t = scratch(4096 + 256, [2, P])
        glu_o = scratch(4096 + 512, [2, P])
        probs = scratch(0, [2, HEADS, SEQ])
        aT = scratch(2048, [2, HEADS, P])
        o_sq = scratch(3072, [HEADS * P])
        o_rs = scratch(3584, [HEADS * P])

        bank = [ctx.enter_context(nc.psum_tensor(f"bank{i}", [P, 512], F32)) for i in range(8)]

        def quad(i):
            return bank[i][:, :].rearrange("p (a t) -> p a t", t=P)

        def score_view(t, m, hd):
            if t == 0:
                return quad(m)[:, hd, :]
            return bank[2 * m + hd // 2][:, SEQ * (hd % 2):SEQ * (hd % 2) + SEQ]

        def col(name, layer, i):
            r0, k = ROW[name]
            c = r0 + layer * k + i
            return pcol[:, c:c + 1]

        s_setup = sem("setup_loaded")
        s_x = sem("x_loaded")
        s_out = sem("out_stored")
        s_w = [sem(f"weights_loaded{i}") for i in range(WRING)]
        s_keys = sem("keys_loaded")
        s_gain = sem("gains_loaded")
        s_row = [sem(f"row_gathered{j}") for j in range(RING)]
        s_used = [sem(f"row_used{j}") for j in range(RING)]
        chunk_done = sem("chunk_multiplied")
        s_pe, s_act, s_dve, s_pool = sem("pe_own"), sem("act_own"), sem("dve_own"), sem("pool_own")
        s_turn = sem("pool_turn")
        s_copied = sem("slot_index_copied")
        st_iota, st_prow, st_pcol, st_ang, st_trig = (sem(f"st_{i}") for i in ("iota", "prow", "pcol", "ang", "trig"))
        st_bd, st_bps, st_done, st_masks, st_cps = (sem(f"st_{i}") for i in ("bd", "bps", "done", "masks", "cps"))
        st_step = sem("st_step")
        x_sd, h_ok, hT_ps, hT_a, hT_v = sem("x_sd"), sem("h_ok"), sem("hT_ps"), sem("hT_a"), sem("hT_v")
        halo, raw_ok, cc_ok = sem("halo"), sem("raw_ok"), sem("cc_ok")
        qk_sq, qk_ss, qk_sd, qk_ok = sem("qk_sq"), sem("qk_ss"), sem("qk_sd"), sem("qk_ok")
        v_ok, qkT_ps, qT_ok, kT_ok = sem("v_ok"), sem("qkT_ps"), sem("qT_ok"), sem("kT_ok")
        lora_a, lora_in, lora_ps, lora_ok = sem("lora_a"), sem("lora_in"), sem("lora_ps"), sem("lora_ok")
        kk_sq, kk_ps, kk_sd, cum_ok, exps = sem("kk_sq"), sem("kk_ps"), sem("kk_sd"), sem("cum_ok"), sem("exps")
        abkr, mats, masked, tr_ps, tok_ok = sem("abkr"), sem("mats"), sem("masked"), sem("tr_ps"), sem("tok_ok")
        ms_ok, pr_ps, pr_ok, up_ps, up_ok = sem("ms_ok"), sem("pr_ps"), sem("pr_ok"), sem("up_ps"), sem("up_ok")
        rhs_ps, rhs_ok, sa_ps, sa_ok, y_ps, y_ok = (sem(i) for i in ("rhs_ps", "rhs_ok", "sa_ps", "sa_ok", "y_ps", "y_ok"))
        mean_ps, dev_ok, var_ps, var_sd, rk_ok, mix_r = (sem(i) for i in ("mean_ps", "dev_ok", "var_ps", "var_sd", "rk_ok", "mix_r"))
        u4_ok, bu_ps, z_ok, xs_ok, sy_ps, sy_ok = sem("u4_ok"), sem("bu_ps"), sem("z_ok"), sem("xs_ok"), sem("sy_ps"), sem("sy_ok")
        gelu_ok, glu_ps, glu_th, glu_sq, gss_ps, gss_sd, mix_s = (sem(i) for i in ("gelu_ok", "glu_ps", "glu_th", "glu_sq", "gss_ps", "gss_sd", "mix_s"))
        sc_ps, max_ok, exp_ok, comb_ok, aT_ps, aT_ok = (sem(i) for i in ("sc_ps", "max_ok", "exp_ok", "comb_ok", "aT_ps", "aT_ok"))
        o_ps, o_sq_ok, oss_ps, oss_sd, mix_d = (sem(i) for i in ("o_ps", "o_sq_ok", "oss_ps", "oss_sd", "mix_d"))
        x_mid = sem("x_mid")
        f_sd, f_h, fT_ps, fT_a, fT_v = sem("f_sd"), sem("f_h"), sem("fT_ps"), sem("fT_a"), sem("fT_v")
        key_ps, key_ok = sem("key_ps"), sem("key_ok")
        pq_ok, ps_ps, ps_ok = sem("pq_ok"), sem("ps_ps"), sem("ps_ok")
        bmax_ok, gexp_ok, ids_ok, dots_ok, act_ok, w_ok = (sem(i) for i in ("bmax_ok", "gexp_ok", "ids_ok", "dots_ok", "act_ok", "w_ok"))
        s_diag = sem("diag_ready")
        y_zero, y_done, ffn_done = sem("y_zero"), sem("y_done"), sem("ffn_done")

        block = ctx.enter_context(nc.Block())
        units = [(n, n // TILES, n % TILES) for n in range(UNITS)]

        def x_input(engine, n):
            if n < TILES:
                engine.wait_ge(s_x, 16 * TILES)
            else:
                engine.wait_ge(ffn_done, n - TILES + 1)

        loads = [0]

        @block.sync
        def _(sp):
            def setup(dst, src):
                sp.dma_start(dst, src).then_inc(s_setup, 16)
                loads[0] += 16

            xv = A["x"][0].rearrange("(t p) d -> t p d", p=P)
            for t in range(TILES):
                sp.dma_start(x[:, t, :], xv[t]).then_inc(s_x, 16)
            for name, k in VECTORS:
                src = A[name]
                flat = src.rearrange({1: "a -> a", 2: "a b -> (a b)", 3: "a b c -> (a b c)"}[len(src.shape)])
                setup(prow[ROW[name][0]:ROW[name][0] + DEPTH * k, :], flat.rearrange("(r c) -> r c", c=P))
            dt_v = A["ssm_log_dt"].rearrange("l (b q) -> q (l b)", q=2)
            for q in range(2):
                with nc.allow_non_contiguous_dma(reason="16 numbers a row"):
                    setup(small[64 * q:64 * q + 64, 0:16], dt_v[q:q + 1, :].broadcast_to([64, 16]))
            with nc.allow_non_contiguous_dma(reason="two numbers a row"):
                setup(ti_pos[:, :], A["positions"].rearrange("a (t p) -> p (a t)", p=P))
            for i, name in enumerate(("ssm_b_re", "ssm_b_im")):
                setup(b_raw[:, i], A[name].rearrange("l (b q) p h -> (q p) (l b) h", q=2))
            for i, name in enumerate(("ssm_c_re", "ssm_c_im")):
                src = A[name].rearrange("l g h p -> (l g h) p").rearrange("(a r) p -> r a p", r=P)
                for dup in range(2):
                    setup(c_raw[:, i, :, 64 * dup:64 * dup + 64], src)
            setup(lam_raw[:, :], A["da_lambda"].rearrange("l a b -> (l a b)").unsqueeze(0).broadcast_to([P, 512]))
            for layer in range(DEPTH):
                setup(glu_w[:, layer], A["ssm_w_glu"][layer].rearrange("(k p) n -> p k n", p=P))
                setup(lora_w[0:32, layer, :], A["rw_decay_up"][layer])
                setup(lora_w[32:64, layer, :], A["rw_aaa_up"][layer])
                setup(lora_w[64:128, layer, :], A["rw_gate_up"][layer])
            g = 0
            for n, layer, t in units:
                w_out_v = A["w_out"][layer].rearrange("(k p) n -> p k n", p=P)
                w_in_v = A["w_in"][layer].rearrange("(k p) n -> p k n", p=P)
                w_q_v = A["peer_w_q"][layer].rearrange("(k p) n -> p k n", p=P)
                if t == 0:
                    if n:
                        sp.wait_ge(qk_ok, n)
                        sp.wait_ge(f_h, n)
                    for i, name in enumerate(("da_q_norm", "da_k_norm")):
                        src = A[name][layer].rearrange("h m d -> (h m d)").unsqueeze(0)
                        sp.dma_start(gain_qk[:, i, :], src.broadcast_to([P, 512])).then_inc(s_gain, 16)
                    sp.dma_start(gain_ffn[:, :], A["norm_ffn"][layer:layer + 1, :].broadcast_to([P, D_MODEL])).then_inc(s_gain, 16)
                    if n:
                        for j in (4, 5):
                            sp.wait_ge(s_used[j], 1 + USES * n)
                    sp.dma_start(keys_raw[:, :, :], A["peer_sub_keys"][layer].rearrange("h m k d -> k (h m) d"))\
                        .then_inc(s_keys, 16)
                for src, chunks in ((w_in_v, BC_CHUNKS + DA_CHUNKS), (w_out_v, OUT_CHUNKS), (w_q_v, Q_CHUNKS)):
                    for c0, width in chunks:
                        if g >= WRING:
                            sp.wait_ge(chunk_done, g - WRING + 1)
                        sp.dma_start(wring[:, g % WRING, :, 0:width], src[:, :, c0:c0 + width])\
                            .then_inc(s_w[g % WRING], 16)
                        g += 1
            ov = out[0].rearrange("(t p) d -> t p d", p=P)
            for t in range(TILES):
                sp.wait_ge(ffn_done, UNITS - TILES + t + 1)
                sp.dma_start(ov[t], x[:, t, :]).then_inc(s_out, 16)
            sp.wait_ge(s_out, 16 * TILES)

        @block.gpsimd
        def _(pool):
            own = Chain(s_pool, pool)
            for j in range(RING):
                pool.sem_inc(s_used[j], 1)
            own.add(nc.gpsimd.iota(ti[:], pattern=[[1, P]], base=0, channel_multiplier=0))
            own.add(nc.gpsimd.memset(zeros[:], 0.0))
            own.add(nc.gpsimd.memset(ones[:], 1.0))
            own.add(nc.gpsimd.memset(u4[:], 0.0))
            own.add(nc.gpsimd.memset(eps[:, 0:1], NORM_EPS))
            own.add(nc.gpsimd.memset(eps[:, 1:2], RW_EPS))
            own.add(nc.gpsimd.memset(cum[:, :, 0:1], 0.0))
            own.add(nc.gpsimd.memset(cT[:], 0.0))
            own.add(nc.gpsimd.memset(bd[:], 0.0))
            pool.wait_ge(s_pool, own.count)
            nc.gpsimd.iota(pi[:], pattern=[[0, P]], base=0, channel_multiplier=1).then_inc(st_iota, 1)
            pool.wait_ge(st_iota, 1)
            tables = {0: A["peer_u"], 1: A["peer_v"]}
            for n, layer, t in units:
                pool.wait_ge(raw_ok, 3 * n + 1)
                if n:
                    pool.wait_ge(bu_ps, 2 * (n - 1) + 2)
                for b in range(4):
                    rs = slice(32 * b, 32 * b + 32)
                    last = nc.gpsimd.tensor_copy(u4[rs, b, :, :], raw[rs, 0:2, 1:P + 1])
                    if b < 3:
                        own.add(last)
                pool.wait_ge(s_pool, own.count)
                last.then_inc(u4_ok, 1)
                pool.wait_ge(u4_ok, n + 1)
                pool.wait_ge(masked, n + 1)
                for k in range(1, LEVELS):
                    if k > 2:
                        pool.wait_ge(pr_ps, NL * n + k - 2)
                    nc.gpsimd.tensor_tensor(ms[k % 2][:, :, :], mT[:, :, :], level[:, k:k + 1, :].broadcast_to([P, HEADS, P]),
                                                     ALU.mult).then_inc(ms_ok, 1)
                    pool.wait_ge(ms_ok, NL * n + k)
                pool.wait_ge(ids_ok, n + 1)
                for kind in range(2):
                    table = tables[kind].rearrange("l e d -> (l e) d")
                    base = USES * n + ROUNDS * kind
                    with pool.Fori(0, ROUNDS) as i:
                        for j in range(RING):
                            pool.wait_ge(s_used[j], i + (base + 1))
                            pool.sem_inc(s_turn, 1)
                            nc.gpsimd.tensor_copy(slot_index[:, j:j + 1], expert[:, bass.ds(i * RING + j, 1)])\
                                .then_inc(s_copied, 1)
                            pool.wait_ge(s_copied, i * RING + (base * RING + j + 1))
                            pool.sem_inc(s_turn, 1)
                            nc.gpsimd.indirect_dma_start(
                                out=rows[j], out_offset=None, in_=table,
                                in_offset=bass.IndirectOffsetOnAxis(ap=slot_index[:, j:j + 1], axis=0),
                            ).then_inc(s_row[j], 16)

        @block.scalar
        def _(act):
            own = Chain(s_act, act)
            A_ = nc.scalar.activation
            act.wait_ge(s_setup, loads[0])
            A_(small[:, 16:32], small[:, 0:16], ACT.Exp).then_inc(st_step, 1)
            act.wait_ge(st_step, 1)
            act.wait_ge(st_ang, 1)
            act.wait_ge(s_act, own.count)
            own.add(A_(mag[:, :], small[:, 32:48], ACT.Exp))
            own.add(A_(small[:, 60:64], small[:, 48:52], ACT.Exp))
            own.add(A_(sn[:, :], ang[:, 0, :], ACT.Sin))
            own.add(A_(cs[:, :], ang[:, 1, :], ACT.Sin))
            act.wait_ge(s_act, own.count)
            A_(small[:, 0:1], eps[:, 0:1], ACT.Copy).then_inc(st_trig, 1)
            act.wait_ge(st_trig, 1)

            def mixing(n, layer, t):
                x_input(act, n)
                own(A_(h[:, :], x[:, t, :], ACT.Square, accum_out=small_m[:, 0:1]))
                A_(small_m[:, 1:2], small_m[:, 0:1], ACT.Sqrt, bias=eps[:, 0:1], scale=1.0 / D_MODEL).then_inc(x_sd, 1)
                act.wait_ge(x_sd, n + 1)
                act.wait_ge(hT_ps, 2 * n + 1)
                for k in range(4):
                    ins = A_(h_cm[:, k, :], quad(0)[:, k, :], ACT.Copy, scale=col("norm_mix", layer, k))
                    if k < 3:
                        own.add(ins)
                act.wait_ge(s_act, own.count)
                ins.then_inc(hT_a, 1)
                act.wait_ge(hT_a, n + 1)
                act.wait_ge(halo, n + 1)
                for j, (b0, nb) in enumerate(((0, 4), (4, 4), (8, 1))):
                    act.wait_ge(chunk_done, CHUNKS * n + BC_DONE[j])
                    A_(raw[:, b0:b0 + nb, 1:P + 1], quad(2 + j)[:, 0:nb, :], ACT.Copy).then_inc(raw_ok, 1)
                    act.wait_ge(raw_ok, 3 * n + j + 1)
                for i in range(2):
                    act.wait_ge(chunk_done, CHUNKS * n + DA_DONE[i])
                    ins = A_(sqs[:, i, :], bank[i][:, :], ACT.Square)
                    if i == 0:
                        own(ins)
                ins.then_inc(qk_sq, 1)
                act.wait_ge(qk_sq, n + 1)
                act.wait_ge(chunk_done, CHUNKS * n + DA_DONE[2])
                A_(v_tok[:, t, :], bank[5][:, :], ACT.Copy).then_inc(v_ok, 1)
                act.wait_ge(v_ok, n + 1)
                act.wait_ge(qk_ss, n + 1)
                A_(small_m[:, 32:48], small_m[:, 16:32], ACT.Sqrt, bias=eps[:, 0:1], scale=1.0 / HD).then_inc(qk_sd, 1)
                act.wait_ge(qk_sd, n + 1)
                act.wait_ge(cc_ok, n + 1)
                own(A_(rw["lora"][0:32, 0, :], cc[0:32, 6, :], ACT.Tanh))
                own(A_(rw["lora"][32:64, 0, :], cc[32:64, 6, :], ACT.Copy))
                A_(rw["lora"][64:128, 0, :], cc[64:128, 6, :], ACT.Tanh, scale=0.5).then_inc(lora_a, 1)
                act.wait_ge(lora_a, n + 1)
                act.wait_ge(lora_ps, n + 1)
                for b in range(2):
                    own.add(A_(rw["ep"][:, b, :], bank[2][:, P * b:P * b + P], ACT.Tanh, scale=0.5,
                               bias=half[:, 2 * layer + b:2 * layer + b + 1]))
                    own.add(A_(rw["a"][:, b, :], bank[3][:, P * b:P * b + P], ACT.Tanh, scale=0.5,
                               bias=half[:, 4 + 2 * layer + b:4 + 2 * layer + b + 1]))
                act.wait_ge(s_act, own.count)
                A_(rw["g"][:, :, :], quad(4)[:, 0:2, :], ACT.Copy).then_inc(lora_ok, 1)
                act.wait_ge(lora_ok, n + 1)
                act.wait_ge(qkT_ps, 2 * n + 1)
                A_(qT[:, :, :], quad(0), ACT.Copy).then_inc(qT_ok, 1)
                act.wait_ge(qT_ok, n + 1)
                act.wait_ge(cum_ok, n + 1)
                for b in range(2):
                    neg_c, c = small_m[:, 4 + b:5 + b], cum[:, b, CHUNK:CHUNK + 1]
                    own.add(A_(rw["ep"][:, b, :], cum[:, b, 1:P + 1], ACT.Exp, bias=neg_c))
                    own.add(A_(rw["em"][:, b, :], cum[:, b, 1:P + 1], ACT.Exp, bias=c, scale=-1.0))
                    own.add(A_(rw["eq"][:, b, :], cum[:, b, 0:P], ACT.Exp, bias=neg_c))
                    own.add(A_(small_m[:, 6 + b:7 + b], c, ACT.Exp))
                act.wait_ge(kk_ps, n + 1)
                act.wait_ge(s_act, own.count)
                A_(rw["rk"][:, :, :], bank[5][:, 0:256].rearrange("p (b t) -> p b t", t=P), ACT.Sqrt).then_inc(kk_sd, 1)
                act.wait_ge(kk_sd, n + 1)
                A_(small_m[:, 8:9], eps[:, 0:1], ACT.Copy).then_inc(exps, 1)
                act.wait_ge(tr_ps, n + 1)
                own.add(A_(tok[:, 0:2, :, :].rearrange("p a b t -> p (a b) t"), quad(4), ACT.Copy))
                act.wait_ge(s_act, own.count)
                A_(tok[:, 2, :, :], quad(5)[:, 0:2, :], ACT.Copy).then_inc(tok_ok, 1)
                act.wait_ge(tok_ok, n + 1)
                for k in range(1, LEVELS):
                    act.wait_ge(pr_ps, NL * n + k)
                    A_(prod[:, :, :], quad(0), ACT.Copy).then_inc(pr_ok, 1)
                    act.wait_ge(pr_ok, NL * n + k)
                act.wait_ge(sa_ps, n + 1)
                A_(sa[:, :, :], bank[2][:, 0:256].rearrange("p (a t) -> p a t", t=HD), ACT.Copy).then_inc(sa_ok, 1)
                act.wait_ge(sa_ok, n + 1)
                act.wait_ge(var_ps, n + 1)
                A_(rw["ep"][:, :, :], quad(1)[:, 0:2, :], ACT.Sqrt, bias=eps[:, 1:2], scale=1.0 / HD).then_inc(var_sd, 1)
                act.wait_ge(var_sd, n + 1)
                act.wait_ge(sy_ok, n + 1)
                A_(yg[:, :, :], glu_t[:, :, :], ACT.Gelu).then_inc(gelu_ok, 1)
                act.wait_ge(gelu_ok, n + 1)
                act.wait_ge(glu_ps, n + 1)
                own(A_(glu_t[:, 0, :], quad(3)[:, 0, :], ACT.Tanh, scale=0.5, bias=half[:, 8 + 2 * layer:9 + 2 * layer]))
                A_(glu_t[:, 1, :], quad(3)[:, 1, :], ACT.Tanh, scale=0.5, bias=half[:, 9 + 2 * layer:10 + 2 * layer]).then_inc(glu_th, 1)
                act.wait_ge(glu_th, n + 1)
                act.wait_ge(gss_ps, n + 1)
                A_(glu_t[:, 0, :], bank[4][:, 0:P], ACT.Sqrt, bias=eps[:, 0:1], scale=1.0 / 256).then_inc(gss_sd, 1)
                act.wait_ge(gss_sd, n + 1)
                kv = P * (t + 1)
                act.wait_ge(max_ok, n + 1)
                for m in range(2):
                    for hd in range(HEADS):
                        i = m * HEADS + hd
                        ins = A_(probs[:, m, hd, 0:kv], score_view(t, m, hd), ACT.Exp, bias=small_a[:, 8 + i:9 + i],
                                 scale=SCALE, accum_out=small_a[:, 16 + i:17 + i])
                        if i < 7:
                            own.add(ins)
                act.wait_ge(s_act, own.count)
                ins.then_inc(exp_ok, 1)
                act.wait_ge(exp_ok, n + 1)
                act.wait_ge(aT_ps, n + 1)
                for c in range(t + 1):
                    ins = A_(aT[:, c, :, :], quad(4 + c), ACT.Copy)
                    if c < t:
                        own.add(ins)
                act.wait_ge(s_act, own.count)
                ins.then_inc(aT_ok, 1)
                act.wait_ge(aT_ok, n + 1)
                act.wait_ge(o_ps, n + 1)
                A_(o_sq[:, :], bank[2][:, :], ACT.Square).then_inc(o_sq_ok, 1)
                act.wait_ge(o_sq_ok, n + 1)
                act.wait_ge(oss_ps, n + 1)
                A_(o_rs[:, :], bank[3][:, :], ACT.Sqrt, bias=eps[:, 0:1], scale=1.0 / P).then_inc(oss_sd, 1)
                act.wait_ge(oss_sd, n + 1)

            def peer(n, layer, t):
                act.wait_ge(x_mid, n + 1)
                own(A_(hb[:, :], x[:, t, :], ACT.Square, accum_out=small_p[:, 0:1]))
                A_(small_p[:, 1:2], small_p[:, 0:1], ACT.Sqrt, bias=eps[:, 0:1], scale=1.0 / D_MODEL).then_inc(f_sd, 1)
                act.wait_ge(f_sd, n + 1)
                act.wait_ge(fT_ps, 2 * n + 1)
                A_(hb_cm[:, 0:4, :], quad(2), ACT.Copy).then_inc(fT_a, 1)
                act.wait_ge(fT_a, n + 1)
                if t == 0:
                    for i in range(4):
                        act.wait_ge(key_ps, 4 * layer + i + 1)
                        A_(keys_cm[:, 4 * i:4 * i + 4, :], quad(4 + i % 2), ACT.Copy).then_inc(key_ok, 1)
                        act.wait_ge(key_ok, 4 * layer + i + 1)
                for i in range(4):
                    act.wait_ge(chunk_done, CHUNKS * n + Q_DONE[i])
                    A_(q_cm[:, 4 * i:4 * i + 4, :], quad(i % 2), ACT.Copy).then_inc(pq_ok, 1)
                    act.wait_ge(pq_ok, 4 * n + i + 1)
                for i in range(4):
                    act.wait_ge(ps_ps, 4 * n + i + 1)
                    A_(scores[:, 4 * i:4 * i + 4, :], quad(2 + i), ACT.Copy).then_inc(ps_ok, 1)
                    act.wait_ge(ps_ok, 4 * n + i + 1)
                act.wait_ge(bmax_ok, n + 1)
                A_(gate[:, :], gate[:, :], ACT.Exp).then_inc(gexp_ok, 1)
                act.wait_ge(gexp_ok, n + 1)
                act.wait_ge(dots_ok, n + 1)
                A_(dots[:, :], dots[:, :], ACT.Gelu).then_inc(act_ok, 1)
                act.wait_ge(act_ok, n + 1)
                act.wait_ge(w_ok, n + 1)
                base = USES * n + ROUNDS
                with act.Fori(0, ROUNDS) as i:
                    for j in range(0, RING, 2):
                        act.wait_ge(s_used[j], i + (base + 1))
                        A_(diag[:, j // 2, :], ident[:, :], ACT.Copy, scale=weight[:, bass.ds(i * RING + j, 1)])\
                            .then_inc(s_diag, 1)

            for n, layer, t in units:
                mixing(n, layer, t)
                peer(n, layer, t)

        @block.vector
        def _(dve):
            V = nc.vector
            own = Chain(s_dve, dve)
            tt, ts, stt = V.tensor_tensor, V.tensor_scalar, V.scalar_tensor_tensor
            dve.wait_ge(st_iota, 1)
            own(tt(xi[:], ti[:], pi[:], ALU.bitwise_xor))
            own.add(tt(ident[:], ti[:], pi[:], ALU.is_equal))
            own.add(tt(strict[:], ti[:], pi[:], ALU.is_gt))
            own.add(tt(incl[:], ti[:], pi[:], ALU.is_ge))
            own.add(tt(lower0[:], ti[:], pi[:], ALU.is_lt))
            own.add(V.tensor_copy(ramp[:], ti[:, 0:TOPK]))
            for k in range(LEVELS):
                own(ts(mask_i[:, k, :], xi[:], k, None, ALU.logical_shift_right))
                own(ts(level[:, k, :], mask_i[:, k, :], 1.0, None, ALU.is_equal))
            own(ts(head_ones[:], mask_i[:, 6, :], 0.0, None, ALU.is_equal))
            own(tt(lower0[:], lower0[:], level[:, 0, :], ALU.mult))
            own(tt(level[:, :, :], level[:, :, :], strict[:, :].unsqueeze(1).broadcast_to([P, LEVELS, P]), ALU.mult))
            V.tensor_copy(small_p[:, 0:1], ident[:, 0:1]).then_inc(st_masks, 1)
            dve.wait_ge(st_masks, 1)
            dve.wait_ge(s_setup, loads[0])
            dve.wait_ge(st_prow, 1)
            own(V.tensor_copy(pcol[:], bank[0][:, 0:NROWS]))
            re0, im0 = ROW["ssm_lambda_re"][0], ROW["ssm_lambda_im"][0]
            w0c = ROW["rw_decay_w0"][0]
            own.add(ts(half[:, 0:12], pcol[:, w0c:w0c + 12], 0.5, None, ALU.mult))
            for layer in range(DEPTH):
                own.add(ts(subln[:, layer:layer + 1], col("da_subln", layer, 0), 1.0 - LAM_INIT[layer], None, ALU.mult))
            lr, li, step = lrt[:, :], pcol[:, im0:im0 + 16], small[:, 16:32]
            own(ts(lr, pcol[:, re0:re0 + 16], -1e-4, None, ALU.min))
            own(tt(lam_raw4[:, :, 0, :], lam_raw4[:, :, 0, :], lam_raw4[:, :, 1, :], ALU.mult))
            own(V.tensor_reduce(small[:, 48:52], lam_raw4[:, :, 0, :], AX.X, ALU.add))
            dve.wait_ge(st_step, 1)
            own(tt(small[:, 32:48], lr, step, ALU.mult))
            own(tt(ang[:, 0, 0:16], li, step, ALU.mult))
            own(V.tensor_copy(posf[:], ti_pos[:]))
            for j in range(ROT):
                own.add(ts(ang[:, 0, 16:32].rearrange("p (t j) -> p t j", j=ROT)[:, :, j], posf[:, :], float(INV_FREQ[j]), None, ALU.mult))
            dve.wait_ge(s_dve, own.count)
            a0, a1 = ang[:, 0, :], ang[:, 1, :]
            own(ts(a1, a0, 1.0 / (2 * math.pi), ROUNDER, ALU.mult, ALU.add))
            own(ts(a1, a1, -ROUNDER, None, ALU.add))
            own(stt(a0, a1, -TWO_PI_A, a0, ALU.mult, ALU.add))
            own(stt(a0, a1, -TWO_PI_B, a0, ALU.mult, ALU.add))
            own(stt(a0, a1, -TWO_PI_C, a0, ALU.mult, ALU.add))
            own(ts(a0, a0, PI_IN, -PI_IN, ALU.min, ALU.max))
            own(stt(a1, a0, -1.0, a0, ALU.mult, ALU.min))
            ts(a1, a1, math.pi / 2, None, ALU.add).then_inc(st_ang, 1)
            dve.wait_ge(st_ang, 1)
            dve.wait_ge(st_trig, 1)
            for layer in range(DEPTH):
                own(tt(neg_lam[:, layer:layer + 1], small[:, 61 + 2 * layer:62 + 2 * layer], small[:, 60 + 2 * layer:61 + 2 * layer], ALU.subtract))
                own(ts(neg_lam[:, layer:layer + 1], neg_lam[:, layer:layer + 1], -LAM_INIT[layer], None, ALU.add))
            are, aim, den, cr, ci, tmp = (s5p[:, i, :] for i in range(6))
            own.add(tt(are, mag[:], cs[:, 0:16], ALU.mult))
            own(tt(aim, mag[:], sn[:, 0:16], ALU.mult))
            own(ts(are, are, -1.0, None, ALU.add))
            own.add(tt(den, lr, lr, ALU.mult))
            own(tt(tmp, li, li, ALU.mult))
            own(tt(den, den, tmp, ALU.add))
            own(V.reciprocal(den, den))
            own.add(tt(cr, are, lr, ALU.mult))
            own(tt(tmp, aim, li, ALU.mult))
            own(tt(cr, cr, tmp, ALU.add))
            own.add(tt(cr, cr, den, ALU.mult))
            own.add(tt(ci, aim, lr, ALU.mult))
            own(tt(tmp, are, li, ALU.mult))
            own(tt(ci, ci, tmp, ALU.subtract))
            own(tt(ci, ci, den, ALU.mult))
            crb, cib = (a.unsqueeze(2).broadcast_to([P, 16, GCH]) for a in (cr, ci))
            own.add(tt(b_t[:, 0], crb, b_raw[:, 0], ALU.mult))
            own.add(tt(b_t[:, 1], cib, b_raw[:, 1], ALU.mult))
            own.add(tt(b_t[:, 2], crb, b_raw[:, 1], ALU.mult))
            own.add(tt(b_t[:, 3], cib, b_raw[:, 0], ALU.mult))
            dve.wait_ge(s_dve, own.count)
            for ri, op in ((0, ALU.subtract), (1, ALU.add)):
                for q in range(2):
                    ps_ = slice(64 * q, 64 * q + 64)
                    dst = bd[ps_, :, ri, :].rearrange("p a (b c) -> p a b c", c=32)[:, :, :, 16 * q:16 * q + 16]
                    own.add(tt(dst, b_t[ps_, 2 * ri].rearrange("p (a b) c -> p a b c", b=4),
                               b_t[ps_, 2 * ri + 1].rearrange("p (a b) c -> p a b c", b=4), op))
            dve.wait_ge(s_dve, own.count)
            V.tensor_copy(small_p[:, 0:1], ident[:, 0:1]).then_inc(st_bd, 1)
            dve.wait_ge(st_bd, 1)
            own.add(V.tensor_copy(e_cos[:, :, 0], cs[:, 0:16]))
            own(V.tensor_copy(e_sin[:, :, 0], sn[:, 0:16]))
            for k in range(LEVELS):
                m = 1 << k
                cm, sm = (e[:, :, m - 1:m].broadcast_to([P, 16, m]) for e in (e_cos, e_sin))
                own.add(tt(dbl[:, :, 0:m], e_cos[:, :, 0:m], cm, ALU.mult))
                own.add(tt(e_cos[:, :, m:2 * m], e_sin[:, :, 0:m], sm, ALU.mult))
                dve.wait_ge(s_dve, own.count)
                own.add(tt(e_cos[:, :, m:2 * m], dbl[:, :, 0:m], e_cos[:, :, m:2 * m], ALU.subtract))
                dve.wait_ge(s_dve, own.count)
                own.add(tt(dbl[:, :, 0:m], e_cos[:, :, 0:m], sm, ALU.mult))
                own.add(tt(e_sin[:, :, m:2 * m], e_sin[:, :, 0:m], cm, ALU.mult))
                dve.wait_ge(s_dve, own.count)
                own(tt(e_sin[:, :, m:2 * m], dbl[:, :, 0:m], e_sin[:, :, m:2 * m], ALU.add))
            dve.wait_ge(st_bps, 1)
            for i in range(2):
                own.add(V.tensor_copy(bT[:, 2 * i:2 * i + 2, :, :].rearrange("p a b c -> p (a b) c"), quad(1 + i)))
            for a in range(2 * DEPTH):
                layer, hb_ = a // 2, a % 2
                for ri in range(2):
                    src = quad(3 + a // 2)[:, 2 * (a % 2) + ri, :].rearrange("p (b q c) -> p b q c", q=2, c=GCH)
                    for q in range(2):
                        ps_ = slice(64 * q, 64 * q + 64)
                        own.add(ts(cT[ps_, layer, 4 * hb_:4 * hb_ + 4, ri, 16 * q:16 * q + 16], src[ps_, :, q, :],
                                   -1.0 if ri else 1.0, None, ALU.mult))
            dve.wait_ge(s_dve, own.count)
            V.tensor_copy(small_p[:, 0:1], ident[:, 0:1]).then_inc(st_done, 1)
            dve.wait_ge(st_done, 1)

            def mixing(n, layer, t):
                if t == 0:
                    V.memset(raw[:, 2:BLOCKS, 0:1], 0.0).then_inc(halo, 1)
                    dve.wait_ge(halo, n + 1)
                else:
                    V.tensor_copy(raw[:, 2:BLOCKS, 0:1], raw[:, 2:BLOCKS, P:P + 1]).then_inc(halo, 1)
                    dve.wait_ge(halo, n + 1)
                dve.wait_ge(x_sd, n + 1)
                own(V.reciprocal(small_m[:, 2:3], small_m[:, 1:2]))
                ts(h[:, :], x[:, t, :], small_m[:, 2:3], None, ALU.mult).then_inc(h_ok, 1)
                dve.wait_ge(h_ok, n + 1)
                dve.wait_ge(hT_ps, 2 * n + 2)
                for k in range(4, 8):
                    ins = ts(h_cm[:, k, :], quad(1)[:, k - 4, :], col("norm_mix", layer, k), None, ALU.mult)
                    if k < 7:
                        own.add(ins)
                ins.then_inc(hT_v, 1)
                dve.wait_ge(hT_v, n + 1)
                dve.wait_ge(raw_ok, 3 * n + 3)
                own(tt(cc[:, :, :], raw[:, 2:BLOCKS, 0:P], raw[:, 2:BLOCKS, 1:P + 1], ALU.subtract))
                for b in range(7):
                    ins = stt(cc[:, b, :], cc[:, b, :], col("rw_mu", layer, b), raw[:, 2 + b, 1:P + 1], ALU.mult, ALU.add)
                    if b < 6:
                        own.add(ins)
                dve.wait_ge(s_dve, own.count)
                ins.then_inc(cc_ok, 1)
                dve.wait_ge(cc_ok, n + 1)
                dve.wait_ge(qk_sq, n + 1)
                V.tensor_reduce(small_m[:, 16:32], sqs[:, :, :].rearrange("p a (b d) -> p (a b) d", d=HD), AX.X, ALU.add).then_inc(qk_ss, 1)
                dve.wait_ge(qk_ss, n + 1)
                dve.wait_ge(qk_sd, n + 1)
                own(V.reciprocal(small_m[:, 32:48], small_m[:, 32:48]))
                for i in range(2):
                    r8 = small_m[:, 32 + 8 * i:40 + 8 * i].unsqueeze(2).broadcast_to([P, 8, HD])
                    own.add(tt(qk[:, i, :].rearrange("p (b d) -> p b d", d=HD), bank[i][:, :].rearrange("p (b d) -> p b d", d=HD), r8, ALU.mult))
                dve.wait_ge(s_dve, own.count)
                dve.wait_ge(s_gain, 48 * (layer + 1))
                own(tt(qk[:, :, :], qk[:, :, :], gain_qk[:, :, :], ALU.mult))
                r = qk[:, :, :].rearrange("p a (b d) -> p (a b) d", d=HD)
                r1, r2 = r[:, :, 0:ROT], r[:, :, ROT:2 * ROT]
                c8, s8 = (a[:, 16 + ROT * t:16 + ROT * t + ROT].unsqueeze(1).broadcast_to([P, 16, ROT]) for a in (cs, sn))
                own.add(tt(qk_tmp[:, 0], r1, c8, ALU.mult))
                own.add(tt(qk_tmp[:, 1], r2, s8, ALU.mult))
                own.add(tt(qk_tmp[:, 2], r2, c8, ALU.mult))
                own.add(tt(qk_tmp[:, 3], r1, s8, ALU.mult))
                dve.wait_ge(s_dve, own.count)
                own.add(tt(r1, qk_tmp[:, 0], qk_tmp[:, 1], ALU.subtract))
                dve.wait_ge(s_dve, own.count)
                tt(r2, qk_tmp[:, 2], qk_tmp[:, 3], ALU.add).then_inc(qk_ok, 1)
                dve.wait_ge(qk_ok, n + 1)
                dve.wait_ge(lora_a, n + 1)
                ts(rw["lora"][64:128, 0, :], rw["lora"][64:128, 0, :], 0.5, 0.5, ALU.mult, ALU.add).then_inc(lora_in, 1)
                dve.wait_ge(lora_in, n + 1)
                rr, kk_, vv = cc[:, 0:2, :], cc[:, 2:4, :], cc[:, 4:6, :]
                for b in range(2):
                    own.add(ts(rw["kk"][:, b, :], kk_[:, b, :], col("rw_k_k", layer, b), None, ALU.mult))
                dve.wait_ge(s_dve, own.count)
                tt(rw["k2"][:, :, :], rw["kk"][:, :, :], rw["kk"][:, :, :], ALU.mult).then_inc(kk_sq, 1)
                dve.wait_ge(kk_sq, n + 1)
                dve.wait_ge(lora_ok, n + 1)
                own.add(ts(rw["a"][:, :, :], rw["a"][:, :, :], 0.5, 0.5, ALU.mult, ALU.add))
                own(ts(rw["ep"][:, :, :], rw["ep"][:, :, :], -0.5 * C_DECAY, -0.5 * C_DECAY, ALU.mult, ALU.add))
                for b in range(2):
                    own.add(V.tensor_tensor_scan(cum[:, b, 1:P + 1], ones[:, :], rw["ep"][:, b, :], 0.0, ALU.mult, ALU.add))
                dve.wait_ge(s_dve, own.count)
                ts(small_m[:, 4:6], cum[:, :, CHUNK], -1.0, None, ALU.mult).then_inc(cum_ok, 1)
                dve.wait_ge(cum_ok, n + 1)
                dve.wait_ge(qkT_ps, 2 * n + 2)
                V.tensor_copy(kT[:, :, P * t:P * t + P], quad(1)).then_inc(kT_ok, 1)
                dve.wait_ge(kT_ok, n + 1)
                dve.wait_ge(kk_sd, n + 1)
                own(ts(rw["rk"][:, :, :], rw["rk"][:, :, :], 1e-12, None, ALU.max))
                own(V.reciprocal(rw["rk"][:, :, :], rw["rk"][:, :, :]))
                own(tt(rw["kk"][:, :, :], rw["kk"][:, :, :], rw["rk"][:, :, :], ALU.mult))
                dve.wait_ge(exps, n + 1)
                own.add(stt(rw["al"][:, :, :], rw["kk"][:, :, :], -1.0, rw["eq"][:, :, :], ALU.mult, ALU.mult))
                own(tt(rw["bm"][:, :, :], rw["kk"][:, :, :], rw["a"][:, :, :], ALU.mult))
                own.add(tt(rw["bm"][:, :, :], rw["bm"][:, :, :], rw["em"][:, :, :], ALU.mult))
                for b in range(2):
                    own.add(ts(rw["k2"][:, b, :], rw["a"][:, b, :], -1.0, col("rw_k_a", layer, b), ALU.add, ALU.mult))
                dve.wait_ge(s_dve, own.count)
                own(stt(rw["k2"][:, :, :], rw["k2"][:, :, :], 1.0, kk_, ALU.add, ALU.mult))
                own.add(tt(rw["km"][:, :, :], rw["k2"][:, :, :], rw["em"][:, :, :], ALU.mult))
                own.add(tt(rw["rp"][:, :, :], rr, rw["ep"][:, :, :], ALU.mult))
                own(tt(rw["k2"][:, :, :], rw["k2"][:, :, :], rr, ALU.mult))
                for b in range(2):
                    own.add(ts(rw["rk"][:, b, :], rw["k2"][:, b, :], col("rw_r_k", layer, b), None, ALU.mult))
                if t == 0:
                    own(V.memset(state[:], 0.0))
                for b in range(2):
                    own.add(ts(state0[:, b, :], state[:, b, :], small_m[:, 6 + b:7 + b], None, ALU.mult))
                own.add(V.tensor_copy(small_m[:, 10:12], rw["ep"][:, :, P - 1]))
                dve.wait_ge(s_dve, own.count)
                V.tensor_copy(small_m[:, 12:13], eps[:, 0:1]).then_inc(abkr, 1)
                dve.wait_ge(abkr, n + 1)
                dve.wait_ge(mats, n + 1)
                for par in range(2):
                    hs = slice(2 * par, 2 * par + 2)

                    def masked_by(dst, src, mask):
                        own.add(tt(dst[:, hs, :], src, mask.unsqueeze(1).broadcast_to([P, 2, P]), ALU.mult))

                    masked_by(mT, quad(0 + par)[:, 0:2, :], strict[:, :])
                    masked_by(inv, quad(0 + par)[:, 2:4, :], lower0[:, :])
                    masked_by(nT, quad(2 + par)[:, 0:2, :], strict[:, :])
                    masked_by(rbT, quad(2 + par)[:, 2:4, :], incl[:, :])
                    masked_by(rkT, quad(4 + par)[:, 0:2, :], incl[:, :])
                dve.wait_ge(s_dve, own.count)
                ib = ident[:, :].unsqueeze(1).broadcast_to([P, HEADS, P])
                own.add(tt(inv[:, :, :], inv[:, :, :], ib, ALU.add))
                own(tt(invT[:, :, :], mT[:, :, :], level[:, 0:1, :].broadcast_to([P, HEADS, P]), ALU.mult))
                tt(invT[:, :, :], invT[:, :, :], ib, ALU.add).then_inc(masked, 1)
                dve.wait_ge(masked, n + 1)
                for k in range(1, LEVELS):
                    dve.wait_ge(up_ps, NL * n + k)
                    if k < LEVELS - 1:
                        own(tt(inv[:, :, :], inv[:, :, :], quad(1), ALU.add))
                    tt(invT[:, :, :], invT[:, :, :], quad(2), ALU.add).then_inc(up_ok, 1)
                    dve.wait_ge(up_ok, NL * n + k)
                dve.wait_ge(rhs_ps, n + 1)
                for par in range(2):
                    ins = V.tensor_copy(rhs[:, 2 * par:2 * par + 2, :], bank[par][:, 0:P].rearrange("p (a t) -> p a t", t=HD))
                    if par == 0:
                        own.add(ins)
                dve.wait_ge(s_dve, own.count)
                ins.then_inc(rhs_ok, 1)
                dve.wait_ge(rhs_ok, n + 1)
                dve.wait_ge(y_ps, n + 1)
                for par in range(2):
                    ps_ = slice(64 * par, 64 * par + 64)
                    own.add(V.tensor_copy(rw["y"][ps_, :, :], quad(3 + par)[ps_, 0:2, :]))
                own(tt(state[:, :, :], state0[:, :, :], bank[5][:, 0:P].rearrange("p (a t) -> p a t", t=HD), ALU.add))
                for b in range(2):
                    own.add(ts(state[:, b, :], state[:, b, :], small_m[:, 10 + b:11 + b], None, ALU.mult))
                dve.wait_ge(s_dve, own.count)
                V.tensor_copy(small_m[:, 12:13], eps[:, 0:1]).then_inc(y_ok, 1)
                dve.wait_ge(y_ok, n + 1)
                dve.wait_ge(mean_ps, n + 1)
                own(stt(rw["y"][:, :, :], quad(0)[:, 0:2, :], -1.0 / HD, rw["y"][:, :, :], ALU.mult, ALU.add))
                tt(rw["kk"][:, :, :], rw["y"][:, :, :], rw["y"][:, :, :], ALU.mult).then_inc(dev_ok, 1)
                dve.wait_ge(dev_ok, n + 1)
                own(tt(rw["k2"][:, :, :], quad(2)[:, 0:2, :], vv, ALU.mult))
                dve.wait_ge(var_sd, n + 1)
                own(V.reciprocal(rw["ep"][:, :, :], rw["ep"][:, :, :]))
                own(tt(rw["y"][:, :, :], rw["y"][:, :, :], rw["ep"][:, :, :], ALU.mult))
                for b in range(2):
                    own.add(ts(rw["y"][:, b, :], rw["y"][:, b, :], col("rw_ln_w", layer, b), col("rw_ln_b", layer, b), ALU.mult, ALU.add))
                dve.wait_ge(s_dve, own.count)
                own(tt(rw["y"][:, :, :], rw["y"][:, :, :], rw["k2"][:, :, :], ALU.add))
                tt(mixed[:, 6:8, :], rw["y"][:, :, :], rw["g"][:, :, :], ALU.mult).then_inc(mix_r, 1)
                dve.wait_ge(mix_r, n + 1)
                for hf in range(2):
                    dve.wait_ge(bu_ps, 2 * n + hf + 1)
                    bs = slice(4 * hf, 4 * hf + 4)
                    ec, es = (e[:, SB * layer + 4 * hf:SB * layer + 4 * hf + 4, :] for e in (e_cos, e_sin))
                    re_, im_ = quad(2 * hf), quad(2 * hf + 1)
                    own.add(tt(zin[0][:, bs, :], re_, ec, ALU.mult))
                    own.add(tt(z[0][:, bs, :], im_, es, ALU.mult))
                    own.add(tt(zin[1][:, bs, :], im_, ec, ALU.mult))
                    own.add(tt(z[1][:, bs, :], re_, es, ALU.mult))
                    dve.wait_ge(s_dve, own.count)
                    own.add(tt(zin[0][:, bs, :], zin[0][:, bs, :], z[0][:, bs, :], ALU.add))
                    dve.wait_ge(s_dve, own.count)
                    tt(zin[1][:, bs, :], zin[1][:, bs, :], z[1][:, bs, :], ALU.subtract).then_inc(z_ok, 1)
                    dve.wait_ge(z_ok, 2 * n + hf + 1)
                for b in range(SB):
                    m = mag[:, SB * layer + b:SB * layer + b + 1].broadcast_to([P, P])
                    for ri in range(2):
                        first = carry[:, ri, b:b + 1] if t else 0.0
                        own.add(V.tensor_tensor_scan(z[ri][:, b, :], m, zin[ri][:, b, :], first, ALU.mult, ALU.add))
                dve.wait_ge(s_dve, own.count)
                ec, es = (e[:, SB * layer:SB * layer + SB, :] for e in (e_cos, e_sin))
                own.add(tt(zin[0][:, :, :], ec, z[0][:, :, :], ALU.mult))
                own.add(tt(zin[1][:, :, :], es, z[1][:, :, :], ALU.mult))
                dve.wait_ge(s_dve, own.count)
                own.add(tt(zin[0][:, :, :], zin[0][:, :, :], zin[1][:, :, :], ALU.subtract))
                dve.wait_ge(s_dve, own.count)
                own.add(tt(zin[1][:, :, :], es, z[0][:, :, :], ALU.mult))
                own.add(tt(z[1][:, :, :], ec, z[1][:, :, :], ALU.mult))
                dve.wait_ge(s_dve, own.count)
                own(tt(zin[1][:, :, :], zin[1][:, :, :], z[1][:, :, :], ALU.add))
                own.add(V.tensor_copy(carry[:, 0, :], zin[0][:, :, P - 1]))
                V.tensor_copy(carry[:, 1, :], zin[1][:, :, P - 1]).then_inc(xs_ok, 1)
                dve.wait_ge(xs_ok, n + 1)
                dve.wait_ge(sy_ps, n + 1)
                for hf in range(2):
                    ins = stt(glu_t[:, hf, :], raw[:, hf, 1:P + 1], col("ssm_d", layer, hf), quad(4)[:, hf, :], ALU.mult, ALU.add)
                    if hf == 0:
                        own.add(ins)
                dve.wait_ge(s_dve, own.count)
                ins.then_inc(sy_ok, 1)
                dve.wait_ge(sy_ok, n + 1)
                dve.wait_ge(glu_th, n + 1)
                own(ts(glu_t[:, :, :], glu_t[:, :, :], 0.5, 0.5, ALU.mult, ALU.add))
                own(tt(glu_o[:, :, :], glu_t[:, :, :], yg[:, :, :], ALU.mult))
                tt(yg[:, :, :], glu_o[:, :, :], glu_o[:, :, :], ALU.mult).then_inc(glu_sq, 1)
                dve.wait_ge(glu_sq, n + 1)
                dve.wait_ge(gss_sd, n + 1)
                own(V.reciprocal(glu_t[:, 0, :], glu_t[:, 0, :]))
                for hf in range(2):
                    ins = stt(mixed[:, 4 + hf, :], glu_o[:, hf, :], col("ssm_out_norm", layer, hf), glu_t[:, 0, :], ALU.mult, ALU.mult)
                    if hf == 0:
                        own.add(ins)
                dve.wait_ge(s_dve, own.count)
                ins.then_inc(mix_s, 1)
                dve.wait_ge(mix_s, n + 1)
                dve.wait_ge(sc_ps, n + 1)
                kv = P * (t + 1)
                nb = 2 * (t + 1)
                per = 8 // nb
                for i in range(nb):
                    own.add(V.memset(bank[i][0:CHUNK, :].rearrange("p (a k) -> p a k", k=kv)[:, :, kv - CHUNK:kv], -1e30))
                dve.wait_ge(s_dve, own.count)
                for i in range(nb):
                    own.add(V.tensor_reduce(small_a[:, per * i:per * i + per], bank[i][:, :].rearrange("p (a k) -> p a k", k=kv), AX.X, ALU.max))
                dve.wait_ge(s_dve, own.count)
                ts(small_a[:, 8:16], small_a[:, 0:8], -SCALE, None, ALU.mult).then_inc(max_ok, 1)
                dve.wait_ge(max_ok, n + 1)
                dve.wait_ge(exp_ok, n + 1)
                own(V.reciprocal(small_a[:, 16:24], small_a[:, 16:24]))
                own(ts(small_a[:, 20:24], small_a[:, 20:24], neg_lam[:, layer:layer + 1], None, ALU.mult))
                for hd in range(HEADS):
                    own.add(ts(probs[:, 0, hd, 0:kv], probs[:, 0, hd, 0:kv], small_a[:, 16 + hd:17 + hd], None, ALU.mult))
                dve.wait_ge(s_dve, own.count)
                for hd in range(HEADS):
                    ins = stt(probs[:, 0, hd, 0:kv], probs[:, 1, hd, 0:kv], small_a[:, 20 + hd:21 + hd], probs[:, 0, hd, 0:kv], ALU.mult, ALU.add)
                    if hd < HEADS - 1:
                        own.add(ins)
                dve.wait_ge(s_dve, own.count)
                ins.then_inc(comb_ok, 1)
                dve.wait_ge(comb_ok, n + 1)
                dve.wait_ge(oss_sd, n + 1)
                own(V.reciprocal(o_rs[:, :], o_rs[:, :]))
                stt(mixed[:, 0:4, :].rearrange("p a t -> p (a t)"), bank[2][:, :], subln[:, layer:layer + 1], o_rs[:, :], ALU.mult, ALU.mult).then_inc(mix_d, 1)
                dve.wait_ge(mix_d, n + 1)
                for i in range(2):
                    dve.wait_ge(chunk_done, CHUNKS * n + OUT_DONE[i])
                    ins = tt(x[:, t, 512 * i:512 * i + 512], x[:, t, 512 * i:512 * i + 512], bank[i][:, :], ALU.add)
                    if i == 0:
                        own.add(ins)
                dve.wait_ge(s_dve, own.count)
                ins.then_inc(x_mid, 1)
                dve.wait_ge(x_mid, n + 1)

            def peer(n, layer, t):
                dve.wait_ge(f_sd, n + 1)
                own(V.reciprocal(small_p[:, 2:3], small_p[:, 1:2]))
                stt(hb[:, :], x[:, t, :], small_p[:, 2:3], gain_ffn[:, :], ALU.mult, ALU.mult).then_inc(f_h, 1)
                dve.wait_ge(f_h, n + 1)
                dve.wait_ge(fT_ps, 2 * n + 2)
                V.tensor_copy(hb_cm[:, 4:8, :], quad(3)).then_inc(fT_v, 1)
                dve.wait_ge(fT_v, n + 1)
                dve.wait_ge(ps_ok, 4 * n + 4)
                for b in range(HM):
                    own.add(V.max(tops[:, b, 0:8], scores[:, b, :]))
                dve.wait_ge(s_dve, own.count)
                for b in range(HM):
                    own.add(V.max_index(topi[:, b, 0:8], tops[:, b, 0:8], scores[:, b, :]))
                dve.wait_ge(s_dve, own.count)
                for b in range(HM):
                    own.add(V.match_replace(scores[:, b, :], tops[:, b, 0:8], scores[:, b, :], -3e38))
                dve.wait_ge(s_dve, own.count)
                for b in range(HM):
                    own.add(V.max(tops[:, b, 8:16], scores[:, b, :]))
                dve.wait_ge(s_dve, own.count)
                for b in range(HM):
                    own.add(V.max_index(topi[:, b, 8:16], tops[:, b, 8:16], scores[:, b, :]))
                dve.wait_ge(s_dve, own.count)
                for hd in range(PEER_HEADS):
                    a = tops[:, 2 * hd, :].unsqueeze(2).broadcast_to([P, TOPK, TOPK])
                    b = tops[:, 2 * hd + 1, :].unsqueeze(1).broadcast_to([P, TOPK, TOPK])
                    own.add(tt(cand[:, hd, :].rearrange("p (a b) -> p a b", b=TOPK), a, b, ALU.add))
                dve.wait_ge(s_dve, own.count)
                for hd in range(PEER_HEADS):
                    own.add(V.max(best[:, hd, 0:8], cand[:, hd, :]))
                dve.wait_ge(s_dve, own.count)
                for hd in range(PEER_HEADS):
                    own.add(V.max_index(bpos[:, hd, 0:8], best[:, hd, 0:8], cand[:, hd, :]))
                dve.wait_ge(s_dve, own.count)
                for hd in range(PEER_HEADS):
                    own.add(V.match_replace(cand[:, hd, :], best[:, hd, 0:8], cand[:, hd, :], -3e38))
                dve.wait_ge(s_dve, own.count)
                for hd in range(PEER_HEADS):
                    own.add(V.max(best[:, hd, 8:16], cand[:, hd, :]))
                dve.wait_ge(s_dve, own.count)
                for hd in range(PEER_HEADS):
                    own.add(V.max_index(bpos[:, hd, 8:16], best[:, hd, 8:16], cand[:, hd, :]))
                dve.wait_ge(s_dve, own.count)
                g3 = gate[:, :].rearrange("p (a b) -> p a b", b=TOPK)
                tt(g3, best[:, :, :], best[:, :, 0:1].broadcast_to([P, PEER_HEADS, TOPK]), ALU.subtract).then_inc(bmax_ok, 1)
                dve.wait_ge(bmax_ok, n + 1)
                own.add(V.tensor_copy(topf[:, :, :], topi[:, :, :]))
                own.add(ts(bhi[:, :, :], bpos[:, :, :], 4, None, ALU.logical_shift_right))
                dve.wait_ge(s_dve, own.count)
                own.add(V.tensor_copy(fhi[:, :], bhi[:, :, :].rearrange("p a b -> p (a b)")))
                own.add(ts(bpos[:, :, :], bpos[:, :, :], 15, None, ALU.bitwise_and))
                dve.wait_ge(s_dve, own.count)
                own(V.tensor_copy(flo[:, :], bpos[:, :, :].rearrange("p a b -> p (a b)")))
                for m, f in ((0, fhi), (1, flo)):
                    own(tt(picked[:, :, :], f[:, :].unsqueeze(2).broadcast_to([P, SLOTS, TOPK]),
                           ramp[:, :].unsqueeze(1).broadcast_to([P, SLOTS, TOPK]), ALU.is_equal))
                    ids = topf[:, :, :].rearrange("p (a m) c -> p a m c", m=2)[:, :, m:m + 1, :].broadcast_to([P, PEER_HEADS, TOPK, TOPK])
                    p4 = picked[:, :, :].rearrange("p (a b) c -> p a b c", b=TOPK)
                    own(tt(p4, p4, ids, ALU.mult))
                    own(V.tensor_reduce(f[:, :], picked[:, :, :], AX.X, ALU.add))
                own(ts(fhi[:, :], fhi[:, :], float(NKEYS), float(layer * N_EXPERTS), ALU.mult, ALU.add))
                tt(expert[:, :], fhi[:, :], flo[:, :], ALU.add).then_inc(ids_ok, 1)
                dve.wait_ge(ids_ok, n + 1)
                dve.wait_ge(gexp_ok, n + 1)
                own(V.tensor_reduce(small_p[:, 8:16], g3, AX.X, ALU.add))
                own(V.reciprocal(small_p[:, 8:16], small_p[:, 8:16]))
                own(tt(g3, g3, small_p[:, 8:16].unsqueeze(2).broadcast_to([P, PEER_HEADS, TOPK]), ALU.mult))
                own(V.memset(y_rows[:, :], 0.0))
                base = USES * n
                with dve.Fori(0, ROUNDS) as i:
                    for j in range(RING):
                        dve.wait_ge(s_row[j], i * 16 + 16 * (base + 1))
                        stt(rows[j], rows[j], 1.0, hb[:, :], ALU.mult, ALU.mult,
                            accum_out=dots[:, bass.ds(i * RING + j, 1)]).then_inc(s_used[j], 1)
                for j in range(RING):
                    dve.wait_ge(s_used[j], 1 + base + ROUNDS)
                V.tensor_copy(small_p[:, 4:5], eps[:, 0:1]).then_inc(dots_ok, 1)
                dve.wait_ge(dots_ok, n + 1)
                dve.wait_ge(act_ok, n + 1)
                tt(weight[:, :], gate[:, :], dots[:, :], ALU.mult).then_inc(w_ok, 1)
                dve.wait_ge(w_ok, n + 1)
                base = USES * n + ROUNDS
                with dve.Fori(0, ROUNDS) as i:
                    for j in range(1, RING, 2):
                        dve.wait_ge(s_row[j], i * 16 + 16 * (base + 1))
                        if j > 1:
                            dve.wait_ge(s_used[j - 2], i + (base + 2))
                        else:
                            dve.wait_ge(s_used[RING - 1], i + (base + 1))
                        stt(y_rows[:, :], rows[j], weight[:, bass.ds(i * RING + j, 1)], y_rows[:, :],
                            ALU.mult, ALU.add).then_inc(s_used[j], 1)
                dve.wait_ge(s_used[RING - 1], 1 + base + ROUNDS)
                own(tt(x[:, t, :], x[:, t, :], y_rows[:, :], ALU.add))
                dve.wait_ge(y_done, n + 1)
                own.add(tt(x[:, t, 0:512], x[:, t, 0:512], bank[6][:, :], ALU.add))
                dve.wait_ge(s_dve, own.count)
                tt(x[:, t, 512:1024], x[:, t, 512:1024], bank[7][:, :], ALU.add).then_inc(ffn_done, 1)
                dve.wait_ge(ffn_done, n + 1)

            for n, layer, t in units:
                mixing(n, layer, t)
                peer(n, layer, t)

        @block.tensor
        def _(pe):
            mm, tr = nc.tensor.matmul, nc.tensor.transpose
            pe.wait_ge(st_masks, 1)
            pe.wait_ge(s_setup, loads[0])
            tr(bank[0][:, 0:NROWS], prow[:, :], ident[0:NROWS, 0:NROWS]).then_inc(st_prow, 1)
            pe.wait_ge(st_bd, 1)
            for i in range(4):
                for ri in range(2):
                    tr(quad(1 + i // 2)[:, 2 * (i % 2) + ri, :], bd[:, i, ri, :], ident[:, :])
            for i in range(4):
                for ri in range(2):
                    last = tr(quad(3 + i // 2)[:, 2 * (i % 2) + ri, :], c_raw[:, ri, i, :], ident[:, :])
            last.then_inc(st_bps, 1)
            pe.wait_ge(st_done, 1)
            g = [0]

            def chunk():
                i = g[0]
                pe.wait_ge(s_w[i % WRING], 16 * (i // WRING + 1))
                return wring[:, i % WRING]

            def chunk_used(last):
                last.then_inc(chunk_done, 1)
                g[0] += 1

            def mixing(n, layer, t):
                pe.wait_ge(h_ok, n + 1)
                if n:
                    pe.wait_ge(ffn_done, n)
                for k in range(KD):
                    last = tr(quad(k // 4)[:, k % 4, :], h[:, P * k:P * k + P], ident[:, :])
                    if k % 4 == 3:
                        last.then_inc(hT_ps, 1)
                pe.wait_ge(hT_a, n + 1)
                pe.wait_ge(hT_v, n + 1)
                b = 0
                for c0, width in BC_CHUNKS:
                    w = chunk()
                    for j in range(width // P):
                        for k in range(KD):
                            last = mm(quad(2 + b // 4)[:, b % 4, :], w[:, k, P * j:P * j + P], h_cm[:, k, :], start=k == 0, stop=k == KD - 1)
                        b += 1
                    chunk_used(last)
                for c, (c0, width) in enumerate(DA_CHUNKS):
                    w = chunk()
                    dst = bank[(0, 1, 5)[c // 2]][:, CW * (c % 2):CW * (c % 2) + CW]
                    for k in range(KD):
                        last = mm(dst, h_cm[:, k, :], w[:, k, :], start=k == 0, stop=k == KD - 1)
                    chunk_used(last)
                pe.wait_ge(raw_ok, 3 * n + 3)
                pe.wait_ge(lora_in, n + 1)
                for b in range(2):
                    bs = slice(P * b, P * b + P)
                    mm(bank[2][:, bs], lora_w[0:32, layer, bs], rw["lora"][0:32, 0, :], start=True, stop=True)
                    mm(bank[3][:, bs], lora_w[32:64, layer, bs], rw["lora"][32:64, 0, :], start=True, stop=True)
                    last = mm(bank[4][:, bs], lora_w[64:128, layer, bs], rw["lora"][64:128, 0, :], start=True, stop=True)
                last.then_inc(lora_ps, 1)
                pe.wait_ge(kk_sq, n + 1)
                pe.wait_ge(v_ok, n + 1)
                mm(bank[5][:, 0:256], head_ones[:, :], rw["k2"][:, :, :].rearrange("p b t -> p (b t)"), start=True, stop=True).then_inc(kk_ps, 1)
                pe.wait_ge(qk_ok, n + 1)
                for i in range(2):
                    for hd in range(HEADS):
                        last = tr(quad(i)[:, hd, :], qk[:, i, P * hd:P * hd + P], ident[:, :])
                    last.then_inc(qkT_ps, 1)
                pe.wait_ge(abkr, n + 1)
                pe.wait_ge(qT_ok, n + 1)
                pe.wait_ge(kT_ok, n + 1)
                pe.wait_ge(lora_ok, n + 1)
                pe.wait_ge(kk_sd, n + 1)
                pairs = ((0, 0, "bm", "al"), (0, 2, "al", "bm"), (2, 0, "km", "al"), (2, 2, "bm", "rp"), (4, 0, "km", "rp"))
                for b0, at, left, right in pairs:
                    for par in range(2):
                        ps_ = slice(64 * par, 64 * par + 64)
                        for pr in range(2):
                            last = mm(quad(b0 + par)[:, at + pr, :], rw[left][ps_, pr, :], rw[right][ps_, pr, :], start=True, stop=True)
                last.then_inc(mats, 1)
                pe.wait_ge(masked, n + 1)
                for i, src in enumerate((cc[:, 4:6, :], rw["bm"], rw["km"])):
                    for b in range(2):
                        last = tr(quad(4 + i // 2)[:, 2 * (i % 2) + b, :], src[:, b, :], ident[:, :])
                last.then_inc(tr_ps, 1)
                for k in range(1, LEVELS):
                    pe.wait_ge(ms_ok, NL * n + k)
                    if k > 1:
                        pe.wait_ge(up_ok, NL * n + k - 1)
                    for i in range(HEADS):
                        last = mm(quad(0)[:, i, :], ms[k % 2][:, i, :], inv[:, i, :], start=True, stop=True)
                    last.then_inc(pr_ps, 1)
                    pe.wait_ge(pr_ok, NL * n + k)
                    for i in range(HEADS):
                        if k < LEVELS - 1:
                            mm(quad(1)[:, i, :], invT[:, i, :], prod[:, i, :], start=True, stop=True)
                        last = mm(quad(2)[:, i, :], prod[:, i, :], invT[:, i, :], start=True, stop=True)
                    last.then_inc(up_ps, 1)
                pe.wait_ge(up_ok, NL * n + NL)
                pe.wait_ge(tok_ok, n + 1)
                heads = [(2 * par + pr, par, pr, slice(64 * par, 64 * par + 64)) for par in range(2) for pr in range(2)]
                for i, par, pr, ps_ in heads:
                    dst = bank[par][:, HD * pr:HD * pr + HD]
                    mm(dst, rw["al"][ps_, pr, :], state0[ps_, pr, :], start=True, stop=False)
                    last = mm(dst, nT[:, i, :], tok[:, 0, pr, ps_], start=False, stop=True)
                last.then_inc(rhs_ps, 1)
                pe.wait_ge(rhs_ok, n + 1)
                for i, par, pr, ps_ in heads:
                    last = mm(bank[2][:, HD * i:HD * i + HD], invT[:, i, :], rhs[:, i, :], start=True, stop=True)
                last.then_inc(sa_ps, 1)
                pe.wait_ge(sa_ok, n + 1)
                for i, par, pr, ps_ in heads:
                    dst = quad(3 + par)[ps_, pr, :]
                    mm(dst, state0[ps_, pr, :], rw["rp"][ps_, pr, :], start=True, stop=False)
                    mm(dst, sa[:, i, :], rbT[:, i, :], start=False, stop=False)
                    mm(dst, tok[:, 0, pr, ps_], rkT[:, i, :], start=False, stop=True)
                    dst = bank[5][ps_, HD * pr:HD * pr + HD]
                    mm(dst, tok[:, 1, pr, ps_], sa[:, i, :], start=True, stop=False)
                    last = mm(dst, tok[:, 2, pr, ps_], tok[:, 0, pr, ps_], start=False, stop=True)
                last.then_inc(y_ps, 1)
                pe.wait_ge(y_ok, n + 1)
                mm(bank[2][:, 0:256], head_ones[:, :], rw["rk"][:, :, :].rearrange("p b t -> p (b t)"), start=True, stop=True)
                mm(bank[0][:, 0:256], head_ones[:, :], rw["y"][:, :, :].rearrange("p b t -> p (b t)"), start=True, stop=True).then_inc(mean_ps, 1)
                pe.wait_ge(dev_ok, n + 1)
                mm(bank[1][:, 0:256], head_ones[:, :], rw["kk"][:, :, :].rearrange("p b t -> p (b t)"), start=True, stop=True).then_inc(var_ps, 1)
                pe.wait_ge(u4_ok, n + 1)
                pe.wait_ge(mix_r, n + 1)
                for hf in range(2):
                    for b in range(4):
                        for ri in range(2):
                            last = mm(quad(2 * hf + ri)[:, b, :], bT[:, 2 * layer + hf, ri, :], u4[:, b, hf, :], start=True, stop=True)
                    last.then_inc(bu_ps, 1)
                pe.wait_ge(xs_ok, n + 1)
                for hf in range(2):
                    for b in range(4):
                        for ri in range(2):
                            last = mm(quad(4)[32 * b:32 * b + 32, hf, :], cT[:, layer, 4 * hf + b, ri, :], zin[ri][:, 4 * hf + b, :],
                                      start=ri == 0, stop=ri == 1)
                last.then_inc(sy_ps, 1)
                pe.wait_ge(gelu_ok, n + 1)
                for o in range(2):
                    for k in range(2):
                        last = mm(quad(3)[:, o, :], glu_w[:, layer, k, P * o:P * o + P], yg[:, k, :], start=k == 0, stop=k == 1)
                last.then_inc(glu_ps, 1)
                pe.wait_ge(glu_sq, n + 1)
                for k in range(2):
                    last = mm(bank[4][:, 0:P], ones[:, :], yg[:, k, :], start=k == 0, stop=k == 1)
                last.then_inc(gss_ps, 1)
                pe.wait_ge(mix_s, n + 1)
                kv = P * (t + 1)
                for m in range(2):
                    for hd in range(HEADS):
                        ms_ = slice(64 * m, 64 * m + 64)
                        last = mm(score_view(t, m, hd), qT[ms_, hd, :], kT[ms_, hd, 0:kv], start=True, stop=True)
                last.then_inc(sc_ps, 1)
                pe.wait_ge(comb_ok, n + 1)
                for c in range(t + 1):
                    for hd in range(HEADS):
                        last = tr(quad(4 + c)[:, hd, :], probs[:, 0, hd, P * c:P * c + P], ident[:, :])
                last.then_inc(aT_ps, 1)
                pe.wait_ge(aT_ok, n + 1)
                for hd in range(HEADS):
                    for c in range(t + 1):
                        last = mm(quad(2)[:, hd, :], v_tok[:, c, P * hd:P * hd + P], aT[:, c, hd, :], start=c == 0, stop=c == t)
                last.then_inc(o_ps, 1)
                pe.wait_ge(o_sq_ok, n + 1)
                mm(bank[3][:, :], ones[:, :], o_sq[:, :], start=True, stop=True).then_inc(oss_ps, 1)
                pe.wait_ge(mix_d, n + 1)
                for c, (c0, width) in enumerate(OUT_CHUNKS):
                    w = chunk()
                    for k in range(KD):
                        last = mm(bank[c // 2][:, CW * (c % 2):CW * (c % 2) + CW], mixed[:, k, :], w[:, k, :], start=k == 0, stop=k == KD - 1)
                    chunk_used(last)

            def peer(n, layer, t):
                pe.wait_ge(f_h, n + 1)
                for k in range(KD):
                    last = tr(quad(2 + k // 4)[:, k % 4, :], hb[:, P * k:P * k + P], ident[:, :])
                    if k % 4 == 3:
                        last.then_inc(fT_ps, 1)
                if t == 0:
                    pe.wait_ge(s_keys, 16 * (layer + 1))
                    for i in range(4):
                        if i > 1:
                            pe.wait_ge(key_ok, 4 * layer + i - 1)
                        for b in range(4):
                            last = tr(quad(4 + i % 2)[:, b, :], keys_raw[:, 4 * i + b, :], ident[:, :])
                        last.then_inc(key_ps, 1)
                pe.wait_ge(fT_a, n + 1)
                pe.wait_ge(fT_v, n + 1)
                pe.wait_ge(x_mid, n + 1)
                for c, (c0, width) in enumerate(Q_CHUNKS):
                    w = chunk()
                    if c % 2 == 0 and c >= 4:
                        pe.wait_ge(pq_ok, 4 * n + c // 2 - 1)
                    for j in range(2):
                        b = 2 * (c % 2) + j
                        for k in range(KD):
                            last = mm(quad((c // 2) % 2)[:, b, :], w[:, k, P * j:P * j + P], hb_cm[:, k, :], start=k == 0, stop=k == KD - 1)
                    chunk_used(last)
                pe.wait_ge(key_ok, 4 * layer + 4)
                for i in range(4):
                    pe.wait_ge(pq_ok, 4 * n + i + 1)
                    for b in range(4):
                        last = mm(quad(2 + i)[:, b, :], q_cm[:, 4 * i + b, :], keys_cm[:, 4 * i + b, :], start=True, stop=True)
                    last.then_inc(ps_ps, 1)
                for half_ in range(2):
                    mm(bank[6 + half_][:, :], zeros[:, :], level[:, 0:4, :].rearrange("p a t -> p (a t)"), start=True, stop=False,
                       skip_group_check=True)
                base = USES * n + ROUNDS
                with pe.Fori(0, ROUNDS) as i:
                    for j in range(0, RING, 2):
                        pe.wait_ge(s_diag, i * (RING // 2) + (n * SLOTS // 2 + j // 2 + 1))
                        pe.wait_ge(s_row[j], i * 16 + 16 * (base + 1))
                        mm(bank[6][:, :], diag[:, j // 2, :], arena[:, j, 0:512], start=False, stop=False, skip_group_check=True)
                        mm(bank[7][:, :], diag[:, j // 2, :], arena[:, j, 512:1024], start=False, stop=False, skip_group_check=True)\
                            .then_inc(s_used[j], 1)
                for half_ in range(2):
                    last = mm(bank[6 + half_][:, :], zeros[:, :], level[:, 0:4, :].rearrange("p a t -> p (a t)"), start=False, stop=True,
                              skip_group_check=True)
                last.then_inc(y_done, 1)

            for n, layer, t in units:
                mixing(n, layer, t)
                peer(n, layer, t)


_INS = ['x', 'positions', 'norm_mix', 'w_in', 'da_q_norm', 'da_k_norm', 'da_lambda', 'da_subln', 'ssm_lambda_re',
        'ssm_lambda_im', 'ssm_b_re', 'ssm_b_im', 'ssm_c_re', 'ssm_c_im', 'ssm_d', 'ssm_log_dt', 'ssm_w_glu',
        'ssm_b_glu', 'ssm_out_norm', 'rw_mu', 'rw_decay_up', 'rw_decay_w0', 'rw_aaa_up', 'rw_aaa_a0', 'rw_gate_up',
        'rw_k_k', 'rw_k_a', 'rw_r_k', 'rw_ln_w', 'rw_ln_b', 'w_out', 'norm_ffn', 'peer_w_q', 'peer_sub_keys',
        'peer_u', 'peer_v']


def kernel(**inputs):
    import concourse.bacc as _bacc
    from concourse.bass_utils import run_bass_kernel_spmd as _run

    nc = _bacc.Bacc("TRN2", target_bir_lowering=False, num_devices=1)
    arrays, args = {}, {}
    for name in _INS:
        a = np.ascontiguousarray(inputs[name])
        arrays[f"in_{name}_dram"] = a
        args[name] = nc.dram_tensor(f"in_{name}_dram", a.shape, mybir.dt.from_np(a.dtype), kind="ExternalInput").ap()
    out = nc.dram_tensor("out_0_dram", (1, SEQ, D_MODEL), F32, kind="ExternalOutput").ap()
    build_program(nc, args, out)
    r = _run(nc, [arrays], core_ids=[0])
    return r.results[0]["out_0_dram"]
```

```python
import math
from contextlib import ExitStack

import numpy as np

import concourse.bass as bass
from concourse import mybir

F32 = mybir.dt.float32
I32 = mybir.dt.int32
U32 = mybir.dt.uint32
ALU = mybir.AluOpType
ACT = mybir.ActivationFunctionType
AX = mybir.AxisListType

P = 128
D_MODEL = 1024
SEQ = 256
DEPTH = 2
TILES = SEQ // P
UNITS = DEPTH * TILES
KD = D_MODEL // P
CHUNK = 64
NORM_EPS = 1e-6
RW_EPS = 64e-5
HEADS = 4
HD = 64
DA_COLS = 1536
BLOCKS = 9
GROUPS, STATE, GCH = 16, 64, 16
SB = GROUPS * STATE // P
PEER_HEADS, NKEYS, TOPK = 8, 128, 16
HM = PEER_HEADS * 2
N_EXPERTS = NKEYS * NKEYS
SLOTS = PEER_HEADS * TOPK
RING = 8
ROUNDS = SLOTS // RING
USES = 2 * ROUNDS
CW = 256
WRING = 3
BC_CHUNKS = [(DA_COLS + CW * c, min(CW, BLOCKS * P - CW * c)) for c in range(5)]
DA_CHUNKS = [(CW * c, CW) for c in range(6)]
OUT_CHUNKS = [(CW * c, CW) for c in range(4)]
Q_CHUNKS = [(CW * c, CW) for c in range(8)]
CHUNKS = len(BC_CHUNKS) + len(DA_CHUNKS) + len(OUT_CHUNKS) + 1 + len(Q_CHUNKS)
BC_DONE, DA_DONE = (2, 4, 5), (7, 9, 11)
OUT_DONE, KEYS_DONE, Q_DONE = (13, 15), 16, (18, 20, 22, 24)
ON_PE = [0, 2, 4, 6]
ON_DVE = [j for j in range(RING) if j not in ON_PE]
REST_LOADS = 18
DMA_SCRATCH = 24576
STEPS = 48
ROWS_BY = [6, 11, 20, 27, 34, 40, 46, 52, 59, 67, 74, 80, 86, 93, 99, 104, 110, 117, 122, 128, 133, 136, 141,
           145, 149, 153, 157, 162, 168, 173, 177, 181, 191, 194, 198, 202, 206, 209, 213, 217, 220, 224, 228,
           231, 236, 240, 244, 247]
assert len(ROWS_BY) == STEPS and all(a <= b for a, b in zip(ROWS_BY, ROWS_BY[1:]))
LEVELS = 7
NL = LEVELS - 1
C_DECAY = math.exp(-0.5)
SCALE = HD ** -0.5
ROT = 8
INV_FREQ = (np.float32(500000.0) ** (-np.arange(0, 16, 2, dtype=np.float32) / np.float32(16))).astype(np.float32)
TWO_PI_A = 6.28125
TWO_PI_B = float(np.float32(2 * math.pi - 6.28125))
TWO_PI_C = float(2 * math.pi - 6.28125 - TWO_PI_B)
ROUNDER = 12582912.0
PI_IN = 3.1415925
LAM_INIT = [0.8 - 0.6 * math.exp(-0.3 * layer) for layer in range(DEPTH)]

VECTORS = [("ssm_lambda_re", 8), ("ssm_lambda_im", 8), ("norm_mix", 8), ("rw_mu", 7), ("rw_decay_w0", 2),
           ("rw_aaa_a0", 2), ("ssm_b_glu", 2), ("rw_k_k", 2), ("rw_k_a", 2), ("rw_r_k", 2), ("rw_ln_w", 2),
           ("rw_ln_b", 2), ("ssm_d", 2), ("ssm_out_norm", 2), ("da_subln", 1)]
ROW = {}
_r = 0
for _name, _k in VECTORS:
    ROW[_name] = (_r, _k)
    _r += DEPTH * _k
NROWS = _r


class Chain:

    def __init__(self, sem, engine):
        self.sem, self.engine, self.count = sem, engine, 0

    def add(self, instruction):
        instruction.then_inc(self.sem, 1)
        self.count += 1

    def __call__(self, instruction):
        self.add(instruction)
        self.engine.wait_ge(self.sem, self.count)


def build_program(nc, A, out):
    ctx = ExitStack()
    with ctx:
        def sb(name, shape, dt=F32):
            return ctx.enter_context(nc.sbuf_tensor(name, shape, dt))

        def sem(name):
            return ctx.enter_context(nc.semaphore(name))

        x = sb("x", [P, TILES, D_MODEL])
        wring = sb("wring", [P, WRING, KD, CW])
        arena = sb("arena", [P, RING, D_MODEL])
        rows = [arena[:, j, :] for j in range(RING)]
        work = sb("work", [P, 20 * 256])
        q_cm = work[:, 0:2048].rearrange("p (b t) -> p b t", t=P)
        scores = work[:, 2048:4096].rearrange("p (b t) -> p b t", t=P)
        cand = work[:, 0:2048].rearrange("p (b t) -> p b t", t=256)
        picked = work[:, 2048:4096].rearrange("p (b t) -> p b t", t=TOPK)
        h = sb("h", [P, D_MODEL])
        h_cm = sb("h_cm", [P, KD, P])
        mixed = h_cm
        hb = sb("hb", [P, D_MODEL])
        hb_cm = sb("hb_cm", [P, KD, P])
        y_rows = sb("y_rows", [P, D_MODEL])
        keys_cm = sb("keys_cm", [P, HM, P])
        gain_ffn = sb("gain_ffn", [P, D_MODEL])
        gain_qk = sb("gain_qk", [P, 2, 512])
        prow = sb("prow", [NROWS, P])
        pcol = sb("pcol", [P, NROWS])
        half = sb("half", [P, DEPTH * 6])
        subln = sb("subln", [P, DEPTH])
        neg_lam = sb("neg_lam", [P, DEPTH])
        glu_w = sb("glu_w", [P, DEPTH, 2, 256])
        lora_w = sb("lora_w", [P, DEPTH, 256])
        bT = sb("bT", [P, DEPTH * 2, 2, P])
        cT = sb("cT", [P, DEPTH, SB, 2, 32])
        e_cos = sb("e_cos", [P, SB, P])
        e_sin = sb("e_sin", [P, SB, P])
        mag = sb("mag", [P, DEPTH * SB])
        carry = sb("carry", [P, 2, SB])
        u4 = sb("u4", [P, 4, 2, P])
        raw = sb("raw", [P, BLOCKS, P + 1])
        cc = sb("cc", [P, 7, P])
        kT = sb("kT", [P, HEADS, SEQ])
        qT = sb("qT", [P, HEADS, P])
        v_tok = sb("v_tok", [P, TILES, 512])
        cs = sb("cs", [P, 32])
        sn = sb("sn", [P, 32])
        level = sb("level", [P, LEVELS, P])
        strict = sb("strict", [P, P])
        incl = sb("incl", [P, P])
        lower0 = sb("lower0", [P, P])
        ident = sb("ident", [P, P])
        ones = sb("ones", [P, P])
        head_ones = sb("head_ones", [P, P])
        zeros = sb("zeros", [P, P])
        ramp = sb("ramp", [P, TOPK])
        small = sb("small", [P, 64])
        eps = sb("eps", [P, 2])
        cum = sb("cum", [P, 2, P + 1])
        state = sb("state", [P, 2, HD])
        state0 = sb("state0", [P, 2, HD])
        rw = {name: sb("rw_" + name, [P, 2, P]) for name in
              ("lora", "g", "kk", "a", "al", "bm", "km", "rp", "ep", "em", "eq", "k2", "rk", "y")}
        tops = sb("tops", [P, HM, TOPK])
        topi = work[:, 4096:4352].bitcast(U32).rearrange("p (a b) -> p a b", b=TOPK)
        topf = work[:, 4352:4608].rearrange("p (a b) -> p a b", b=TOPK)
        best = work[:, 4608:4736].rearrange("p (a b) -> p a b", b=TOPK)
        bpos = work[:, 4736:4864].bitcast(U32).rearrange("p (a b) -> p a b", b=TOPK)
        bhi = work[:, 4864:4992].bitcast(U32).rearrange("p (a b) -> p a b", b=TOPK)
        flo = work[:, 4992:5120]
        fhi = sb("fhi", [P, SLOTS])
        expert = sb("expert", [P, 2, SLOTS], I32)
        slot_index = sb("slot_index", [P, RING], I32)
        gate = sb("gate", [P, SLOTS])
        dots = sb("dots", [P, SLOTS])
        weight = sb("weight", [P, SLOTS])
        diag = sb("diag", [P, len(ON_PE), P])

        small_m = sb("small_m", [P, 64])
        small_p = sb("small_p", [P, 32])
        small_a = sb("small_a", [P, 32])
        ti_pos = sb("ti_pos", [P, TILES], I32)
        posf = sb("posf", [P, TILES])
        ang = sb("ang", [P, 2, 32])
        lrt = sb("lrt", [P, 16])
        s5p = sb("s5p", [P, 6, 16])
        c_raw = rows[0].rearrange("p (a b c) -> p a b c", a=2, b=4)
        bd = rows[1].rearrange("p (a b c) -> p a b c", a=4, b=2)
        b_raw = rows[2][:, 0:512].rearrange("p (a b c) -> p a b c", a=2, b=16)
        lam_raw = rows[2][:, 512:1024]
        lam_raw4 = lam_raw.rearrange("p (a m d) -> p a m d", m=2, d=HD)
        b_t = rows[3].rearrange("p (a b c) -> p a b c", a=4, b=16)
        ti, pi, xi = (work[:, P * i:P * i + P].bitcast(I32) for i in range(3))
        mask_i = rows[6][:, 0:LEVELS * P].bitcast(I32).rearrange("p (a b) -> p a b", b=P)

        def scratch(at, shape):
            size = int(np.prod(shape))
            view = work[:, at:at + size]
            if len(shape) == 1:
                return view
            names = "abcd"[:len(shape)]
            return view.rearrange(f"p ({' '.join(names)}) -> p {' '.join(names)}",
                                  **{c: s for c, s in zip(names[1:], shape[1:])})

        mT, nT, rbT, rkT = (scratch(512 * i, [HEADS, P]) for i in range(4))
        inv, invT, prod = (scratch(2048 + 512 * i, [HEADS, P]) for i in range(3))
        ms = [scratch(3584 + 512 * i, [HEADS, P]) for i in range(2)]
        sqs = scratch(0, [2, 512])
        qk = scratch(1024, [2, 512])
        qk_tmp = scratch(2048, [4, 16, ROT])
        tok = sb("tok", [P, 3, 2, P])
        rhs = scratch(4608, [HEADS, HD])
        sa = scratch(4864, [HEADS, HD])
        zin = [scratch(1024 * i, [SB, P]) for i in range(2)]
        z = [scratch(2048 + 1024 * i, [SB, P]) for i in range(2)]
        dbl = scratch(4608, [SB, P // 2])
        yg = scratch(4096, [2, P])
        glu_t = scratch(4096 + 256, [2, P])
        glu_o = scratch(4096 + 512, [2, P])
        probs = scratch(0, [2, HEADS, SEQ])
        aT = scratch(2048, [2, HEADS, P])
        o_sq = scratch(3072, [HEADS * P])
        o_rs = scratch(3584, [HEADS * P])

        bank = [ctx.enter_context(nc.psum_tensor(f"bank{i}", [P, 512], F32)) for i in range(8)]

        def quad(i):
            return bank[i][:, :].rearrange("p (a t) -> p a t", t=P)

        def score_view(t, m, hd):
            if t == 0:
                return quad(m)[:, hd, :]
            return bank[2 * m + hd // 2][:, SEQ * (hd % 2):SEQ * (hd % 2) + SEQ]

        def col(name, layer, i):
            r0, k = ROW[name]
            c = r0 + layer * k + i
            return pcol[:, c:c + 1]

        s_setup, s_setup_rest = sem("vectors_loaded"), sem("setup_loaded")
        s_x = sem("x_loaded")
        s_out = sem("out_stored")
        s_w = [sem(f"weights_loaded{i}") for i in range(WRING)]
        s_keys = sem("keys_loaded")
        s_gain = sem("gains_loaded")
        s_row = [sem(f"row_gathered{j}") for j in range(RING)]
        s_used = [sem(f"row_used{j}") for j in range(RING)]
        chunk_done = sem("chunk_multiplied")
        s_pe, s_act, s_dve, s_pool = sem("pe_own"), sem("act_own"), sem("dve_own"), sem("pool_own")
        s_turn = sem("pool_turn")
        s_copied = sem("slot_index_copied")
        st_iota, st_prow, st_pcol, st_ang, st_trig = (sem(f"st_{i}") for i in ("iota", "prow", "pcol", "ang", "trig"))
        st_bd, st_bps, st_done, st_masks, st_cps = (sem(f"st_{i}") for i in ("bd", "bps", "done", "masks", "cps"))
        st_step, st_input = sem("st_step"), sem("st_input")
        x_sd, h_ok, hT_ps, hT_a, hT_v = sem("x_sd"), sem("h_ok"), sem("hT_ps"), sem("hT_a"), sem("hT_v")
        halo, raw_ok, cc_ok = sem("halo"), sem("raw_ok"), sem("cc_ok")
        qk_sq, qk_ss, qk_sd, qk_ok = sem("qk_sq"), sem("qk_ss"), sem("qk_sd"), sem("qk_ok")
        v_ok, qkT_ps, qT_ok, kT_ok = sem("v_ok"), sem("qkT_ps"), sem("qT_ok"), sem("kT_ok")
        lora_a, lora_in, lora_ps, lora_ok = sem("lora_a"), sem("lora_in"), sem("lora_ps"), sem("lora_ok")
        kk_sq, kk_ps, kk_sd, cum_ok, exps = sem("kk_sq"), sem("kk_ps"), sem("kk_sd"), sem("cum_ok"), sem("exps")
        abkr, mats, masked, tr_ps, tok_ok = sem("abkr"), sem("mats"), sem("masked"), sem("tr_ps"), sem("tok_ok")
        ms_ok, pr_ps, pr_ok, up_ps, up_ok = sem("ms_ok"), sem("pr_ps"), sem("pr_ok"), sem("up_ps"), sem("up_ok")
        rhs_ps, rhs_ok, sa_ps, sa_ok, y_ps, y_ok = (sem(i) for i in ("rhs_ps", "rhs_ok", "sa_ps", "sa_ok", "y_ps", "y_ok"))
        mean_ps, dev_ok, var_ps, var_sd, rk_ok, mix_r = (sem(i) for i in ("mean_ps", "dev_ok", "var_ps", "var_sd", "rk_ok", "mix_r"))
        u4_ok, bu_ps, z_ok, xs_ok, sy_ps, sy_ok = sem("u4_ok"), sem("bu_ps"), sem("z_ok"), sem("xs_ok"), sem("sy_ps"), sem("sy_ok")
        gelu_ok, glu_ps, glu_th, glu_sq, gss_ps, gss_sd, mix_s = (sem(i) for i in ("gelu_ok", "glu_ps", "glu_th", "glu_sq", "gss_ps", "gss_sd", "mix_s"))
        sc_ps, max_ok, exp_ok, comb_ok, aT_ps, aT_ok = (sem(i) for i in ("sc_ps", "max_ok", "exp_ok", "comb_ok", "aT_ps", "aT_ok"))
        o_ps, o_sq_ok, oss_ps, oss_sd, mix_d = (sem(i) for i in ("o_ps", "o_sq_ok", "oss_ps", "oss_sd", "mix_d"))
        x_mid = sem("x_mid")
        f_sd, f_h, fT_ps, fT_a, fT_v = sem("f_sd"), sem("f_h"), sem("fT_ps"), sem("fT_a"), sem("fT_v")
        key_ps, key_ok = sem("key_ps"), sem("key_ok")
        pq_ok, ps_ps, ps_ok = sem("pq_ok"), sem("ps_ps"), sem("ps_ok")
        bmax_ok, gexp_ok, ids_ok, dots_ok, act_ok, w_ok = (sem(i) for i in ("bmax_ok", "gexp_ok", "ids_ok", "dots_ok", "act_ok", "w_ok"))
        s_diag = sem("diag_ready")
        y_zero, y_done, ffn_done = sem("y_zero"), sem("y_done"), sem("ffn_done")

        block = ctx.enter_context(nc.Block())
        units = [(n, n // TILES, n % TILES) for n in range(UNITS)]

        def x_input(engine, n):
            if n < TILES:
                engine.wait_ge(s_x, 16 * TILES)
            else:
                engine.wait_ge(ffn_done, n - TILES + 1)

        loads = [0]

        @block.sync
        def _(sp):
            def setup(dst, src):
                sp.dma_start(dst, src).then_inc(s_setup, 16)
                loads[0] += 16

            xv = A["x"][0].rearrange("(t p) d -> t p d", p=P)
            for t in range(TILES):
                sp.dma_start(x[:, t, :], xv[t]).then_inc(s_x, 16)
            for name, k in VECTORS:
                src = A[name]
                flat = src.rearrange({1: "a -> a", 2: "a b -> (a b)", 3: "a b c -> (a b c)"}[len(src.shape)])
                setup(prow[ROW[name][0]:ROW[name][0] + DEPTH * k, :], flat.rearrange("(r c) -> r c", c=P))
            g = 0
            for n, layer, t in units:
                w_out_v = A["w_out"][layer].rearrange("(k p) n -> p k n", p=P)
                w_in_v = A["w_in"][layer].rearrange("(k p) n -> p k n", p=P)
                w_q_v = A["peer_w_q"][layer].rearrange("(k p) n -> p k n", p=P)
                if t == 0:
                    if n:
                        sp.wait_ge(qk_ok, n)
                        sp.wait_ge(f_h, n)
                    for i, name in enumerate(("da_q_norm", "da_k_norm")):
                        src = A[name][layer].rearrange("h m d -> (h m d)").unsqueeze(0)
                        sp.dma_start(gain_qk[:, i, :], src.broadcast_to([P, 512])).then_inc(s_gain, 16)
                    sp.dma_start(gain_ffn[:, :], A["norm_ffn"][layer:layer + 1, :].broadcast_to([P, D_MODEL])).then_inc(s_gain, 16)
                keys_v = A["peer_sub_keys"][layer].rearrange("h m k d -> k (h m) d")
                for src, chunks in ((w_in_v, BC_CHUNKS + DA_CHUNKS), (w_out_v, OUT_CHUNKS), (keys_v, [None]), (w_q_v, Q_CHUNKS)):
                    for c in chunks:
                        if g >= WRING:
                            sp.wait_ge(chunk_done, g - WRING + 1)
                        if c is None:
                            dst, part = wring[:, g % WRING].rearrange("p k (a d) -> p (k a) d", d=P), src
                        else:
                            dst, part = wring[:, g % WRING, :, 0:c[1]], src[:, :, c[0]:c[0] + c[1]]
                        sp.dma_start(dst, part).then_inc(s_w[g % WRING], 16)
                        g += 1
            ov = out[0].rearrange("(t p) d -> t p d", p=P)
            for t in range(TILES):
                sp.wait_ge(ffn_done, UNITS - TILES + t + 1)
                sp.dma_start(ov[t], x[:, t, :]).then_inc(s_out, 16)
            sp.wait_ge(s_out, 16 * TILES)

        @block.gpsimd
        def _(pool):
            own = Chain(s_pool, pool)
            for j in range(RING):
                pool.sem_inc(s_used[j], 1)
            own.add(nc.gpsimd.iota(ti[:], pattern=[[1, P]], base=0, channel_multiplier=0))
            own.add(nc.gpsimd.memset(zeros[:], 0.0))
            own.add(nc.gpsimd.memset(ones[:], 1.0))
            own.add(nc.gpsimd.memset(u4[:], 0.0))
            own.add(nc.gpsimd.memset(eps[:, 0:1], NORM_EPS))
            own.add(nc.gpsimd.memset(eps[:, 1:2], RW_EPS))
            own.add(nc.gpsimd.memset(cum[:, :, 0:1], 0.0))
            own.add(nc.gpsimd.memset(cT[:], 0.0))
            own.add(nc.gpsimd.memset(bd[:], 0.0))
            pool.wait_ge(s_pool, own.count)
            nc.gpsimd.iota(pi[:], pattern=[[0, P]], base=0, channel_multiplier=1).then_inc(st_iota, 1)
            pool.wait_ge(st_iota, 1)
            tables = {0: A["peer_u"], 1: A["peer_v"]}
            for n, layer, t in units:
                pool.wait_ge(ids_ok, n + 1)
                for kind in range(2):
                    table = tables[kind].rearrange("l e d -> (l e) d")
                    base = USES * n + ROUNDS * kind
                    with pool.Fori(0, ROUNDS) as i:
                        for j in range(RING):
                            pool.wait_ge(s_used[j], i + (base + 1))
                            pool.sem_inc(s_turn, 1)
                            nc.gpsimd.tensor_copy(slot_index[:, j:j + 1], expert[:, n % 2, bass.ds(i * RING + j, 1)])\
                                .then_inc(s_copied, 1)
                            pool.wait_ge(s_copied, i * RING + (base * RING + j + 1))
                            pool.sem_inc(s_turn, 1)
                            nc.gpsimd.indirect_dma_start(
                                out=rows[j], out_offset=None, in_=table,
                                in_offset=bass.IndirectOffsetOnAxis(ap=slot_index[:, j:j + 1], axis=0),
                            ).then_inc(s_row[j], 16)

        @block.scalar
        def _(act):
            own = Chain(s_act, act)
            A_ = nc.scalar.activation
            def load(dst, src):
                act.dma_start(dst, src).then_inc(s_setup_rest, 16)
                rest[0] += 1

            rest = [0]
            dt_v = A["ssm_log_dt"].rearrange("l (b q) -> q (l b)", q=2)
            for q in range(2):
                with nc.allow_non_contiguous_dma(reason="16 numbers a row"):
                    load(small[64 * q:64 * q + 64, 0:16], dt_v[q:q + 1, :].broadcast_to([64, 16]))
            with nc.allow_non_contiguous_dma(reason="two numbers a row"):
                load(ti_pos[:, :], A["positions"].rearrange("a (t p) -> p (a t)", p=P))
            for i, name in enumerate(("ssm_b_re", "ssm_b_im")):
                load(b_raw[:, i], A[name].rearrange("l (b q) p h -> (q p) (l b) h", q=2))
            for i, name in enumerate(("ssm_c_re", "ssm_c_im")):
                src = A[name].rearrange("l g h p -> (l g h) p").rearrange("(a r) p -> r a p", r=P)
                for dup in range(2):
                    load(c_raw[:, i, :, 64 * dup:64 * dup + 64], src)
            load(lam_raw[:, :], A["da_lambda"].rearrange("l a b -> (l a b)").unsqueeze(0).broadcast_to([P, 512]))
            for layer in range(DEPTH):
                load(glu_w[:, layer], A["ssm_w_glu"][layer].rearrange("(k p) n -> p k n", p=P))
                load(lora_w[0:32, layer, :], A["rw_decay_up"][layer])
                load(lora_w[32:64, layer, :], A["rw_aaa_up"][layer])
                load(lora_w[64:128, layer, :], A["rw_gate_up"][layer])
            assert rest[0] == REST_LOADS

            act.wait_ge(st_iota, 1)

            def setup_rest():
                act.wait_ge(s_setup_rest, 16 * REST_LOADS)
                A_(small[:, 16:32], small[:, 0:16], ACT.Exp).then_inc(st_step, 1)
                act.wait_ge(st_step, 1)
                act.wait_ge(st_ang, 1)
                act.wait_ge(s_act, own.count)
                own.add(A_(mag[:, :], small[:, 32:48], ACT.Exp))
                own.add(A_(small[:, 60:64], small[:, 48:52], ACT.Exp))
                own.add(A_(sn[:, :], ang[:, 0, :], ACT.Sin))
                own.add(A_(cs[:, :], ang[:, 1, :], ACT.Sin))
                act.wait_ge(s_act, own.count)
                A_(small[:, 0:1], eps[:, 0:1], ACT.Copy).then_inc(st_trig, 1)
                act.wait_ge(st_trig, 1)

            def mixing(n, layer, t):
                x_input(act, n)
                own(A_(h[:, :], x[:, t, :], ACT.Square, accum_out=small_m[:, 0:1]))
                A_(small_m[:, 1:2], small_m[:, 0:1], ACT.Sqrt, bias=eps[:, 0:1], scale=1.0 / D_MODEL).then_inc(x_sd, 1)
                act.wait_ge(x_sd, n + 1)
                yield 0
                act.wait_ge(hT_ps, 2 * n + 1)
                for k in range(4):
                    ins = A_(h_cm[:, k, :], quad(0)[:, k, :], ACT.Copy, scale=col("norm_mix", layer, k))
                    if k < 3:
                        own.add(ins)
                act.wait_ge(s_act, own.count)
                ins.then_inc(hT_a, 1)
                act.wait_ge(hT_a, n + 1)
                if n == 0:
                    setup_rest()
                act.wait_ge(halo, n + 1)
                for j, (b0, nb) in enumerate(((0, 4), (4, 4), (8, 1))):
                    yield 1
                    act.wait_ge(chunk_done, CHUNKS * n + BC_DONE[j])
                    A_(raw[:, b0:b0 + nb, 1:P + 1], quad(2 + j)[:, 0:nb, :], ACT.Copy).then_inc(raw_ok, 1)
                    act.wait_ge(raw_ok, 3 * n + j + 1)
                    if j == 0:
                        for b in range(4):
                            rs = slice(32 * b, 32 * b + 32)
                            ins = A_(u4[rs, b, :, :], raw[rs, 0:2, 1:P + 1], ACT.Copy)
                            if b < 3:
                                own.add(ins)
                        ins.then_inc(u4_ok, 1)
                for i in range(2):
                    act.wait_ge(chunk_done, CHUNKS * n + DA_DONE[i])
                    ins = A_(sqs[:, i, :], bank[i][:, :], ACT.Square)
                    if i == 0:
                        own(ins)
                ins.then_inc(qk_sq, 1)
                act.wait_ge(qk_sq, n + 1)
                act.wait_ge(chunk_done, CHUNKS * n + DA_DONE[2])
                A_(v_tok[:, t, :], bank[5][:, :], ACT.Copy).then_inc(v_ok, 1)
                act.wait_ge(v_ok, n + 1)
                yield 3
                act.wait_ge(qk_ss, n + 1)
                A_(small_m[:, 32:48], small_m[:, 16:32], ACT.Sqrt, bias=eps[:, 0:1], scale=1.0 / HD).then_inc(qk_sd, 1)
                act.wait_ge(qk_sd, n + 1)
                act.wait_ge(cc_ok, n + 1)
                own(A_(rw["lora"][0:32, 0, :], cc[0:32, 6, :], ACT.Tanh))
                own(A_(rw["lora"][32:64, 0, :], cc[32:64, 6, :], ACT.Copy))
                A_(rw["lora"][64:128, 0, :], cc[64:128, 6, :], ACT.Tanh, scale=0.5).then_inc(lora_a, 1)
                act.wait_ge(lora_a, n + 1)
                yield 5
                act.wait_ge(lora_ps, n + 1)
                for b in range(2):
                    own.add(A_(rw["ep"][:, b, :], bank[2][:, P * b:P * b + P], ACT.Tanh, scale=0.5,
                               bias=half[:, 2 * layer + b:2 * layer + b + 1]))
                    own.add(A_(rw["a"][:, b, :], bank[3][:, P * b:P * b + P], ACT.Tanh, scale=0.5,
                               bias=half[:, 4 + 2 * layer + b:4 + 2 * layer + b + 1]))
                act.wait_ge(s_act, own.count)
                A_(rw["g"][:, :, :], quad(4)[:, 0:2, :], ACT.Copy).then_inc(lora_ok, 1)
                act.wait_ge(lora_ok, n + 1)
                act.wait_ge(qkT_ps, 2 * n + 1)
                A_(qT[:, :, :], quad(0), ACT.Copy).then_inc(qT_ok, 1)
                act.wait_ge(qT_ok, n + 1)
                yield 6
                act.wait_ge(cum_ok, n + 1)
                for b in range(2):
                    neg_c, c = small_m[:, 4 + b:5 + b], cum[:, b, CHUNK:CHUNK + 1]
                    own.add(A_(rw["ep"][:, b, :], cum[:, b, 1:P + 1], ACT.Exp, bias=neg_c))
                    own.add(A_(rw["em"][:, b, :], cum[:, b, 1:P + 1], ACT.Exp, bias=c, scale=-1.0))
                    own.add(A_(rw["eq"][:, b, :], cum[:, b, 0:P], ACT.Exp, bias=neg_c))
                    own.add(A_(small_m[:, 6 + b:7 + b], c, ACT.Exp))
                act.wait_ge(kk_ps, n + 1)
                act.wait_ge(s_act, own.count)
                A_(rw["rk"][:, :, :], bank[5][:, 0:256].rearrange("p (b t) -> p b t", t=P), ACT.Sqrt).then_inc(kk_sd, 1)
                act.wait_ge(kk_sd, n + 1)
                A_(small_m[:, 8:9], eps[:, 0:1], ACT.Copy).then_inc(exps, 1)
                yield 9
                act.wait_ge(tr_ps, n + 1)
                own.add(A_(tok[:, 0:2, :, :].rearrange("p a b t -> p (a b) t"), quad(4), ACT.Copy))
                act.wait_ge(s_act, own.count)
                A_(tok[:, 2, :, :], quad(5)[:, 0:2, :], ACT.Copy).then_inc(tok_ok, 1)
                act.wait_ge(tok_ok, n + 1)
                for k in range(1, LEVELS):
                    yield 8 + k
                    act.wait_ge(pr_ps, NL * n + k)
                    A_(prod[:, :, :], quad(0), ACT.Copy).then_inc(pr_ok, 1)
                    yield 8 + k
                    act.wait_ge(pr_ok, NL * n + k)
                yield 16
                act.wait_ge(sa_ps, n + 1)
                A_(sa[:, :, :], bank[2][:, 0:256].rearrange("p (a t) -> p a t", t=HD), ACT.Copy).then_inc(sa_ok, 1)
                act.wait_ge(sa_ok, n + 1)
                yield 18
                act.wait_ge(var_ps, n + 1)
                A_(rw["ep"][:, :, :], quad(1)[:, 0:2, :], ACT.Sqrt, bias=eps[:, 1:2], scale=1.0 / HD).then_inc(var_sd, 1)
                act.wait_ge(var_sd, n + 1)
                yield 23
                act.wait_ge(sy_ok, n + 1)
                A_(yg[:, :, :], glu_t[:, :, :], ACT.Gelu).then_inc(gelu_ok, 1)
                act.wait_ge(gelu_ok, n + 1)
                act.wait_ge(glu_ps, n + 1)
                own(A_(glu_t[:, 0, :], quad(3)[:, 0, :], ACT.Tanh, scale=0.5, bias=half[:, 8 + 2 * layer:9 + 2 * layer]))
                A_(glu_t[:, 1, :], quad(3)[:, 1, :], ACT.Tanh, scale=0.5, bias=half[:, 9 + 2 * layer:10 + 2 * layer]).then_inc(glu_th, 1)
                act.wait_ge(glu_th, n + 1)
                yield 24
                act.wait_ge(gss_ps, n + 1)
                A_(glu_t[:, 0, :], bank[4][:, 0:P], ACT.Sqrt, bias=eps[:, 0:1], scale=1.0 / 256).then_inc(gss_sd, 1)
                act.wait_ge(gss_sd, n + 1)
                kv = P * (t + 1)
                yield 26
                act.wait_ge(max_ok, n + 1)
                for m in range(2):
                    for hd in range(HEADS):
                        i = m * HEADS + hd
                        ins = A_(probs[:, m, hd, 0:kv], score_view(t, m, hd), ACT.Exp, bias=small_a[:, 8 + i:9 + i],
                                 scale=SCALE, accum_out=small_a[:, 16 + i:17 + i])
                        if i < 7:
                            own.add(ins)
                act.wait_ge(s_act, own.count)
                ins.then_inc(exp_ok, 1)
                act.wait_ge(exp_ok, n + 1)
                yield 27
                act.wait_ge(aT_ps, n + 1)
                for c in range(t + 1):
                    ins = A_(aT[:, c, :, :], quad(4 + c), ACT.Copy)
                    if c < t:
                        own.add(ins)
                act.wait_ge(s_act, own.count)
                ins.then_inc(aT_ok, 1)
                act.wait_ge(aT_ok, n + 1)
                act.wait_ge(o_ps, n + 1)
                A_(o_sq[:, :], bank[2][:, :], ACT.Square).then_inc(o_sq_ok, 1)
                act.wait_ge(o_sq_ok, n + 1)
                act.wait_ge(oss_ps, n + 1)
                A_(o_rs[:, :], bank[3][:, :], ACT.Sqrt, bias=eps[:, 0:1], scale=1.0 / P).then_inc(oss_sd, 1)
                act.wait_ge(oss_sd, n + 1)

            def peer(n, layer, t):
                yield 29
                act.wait_ge(x_mid, n + 1)
                own(A_(h[:, :], x[:, t, :], ACT.Square, accum_out=small_p[:, 0:1]))
                A_(small_p[:, 1:2], small_p[:, 0:1], ACT.Sqrt, bias=eps[:, 0:1], scale=1.0 / D_MODEL).then_inc(f_sd, 1)
                act.wait_ge(f_sd, n + 1)
                yield 30
                act.wait_ge(fT_ps, 2 * n + 1)
                A_(hb_cm[:, 0:4, :], quad(2), ACT.Copy).then_inc(fT_a, 1)
                act.wait_ge(fT_a, n + 1)
                for i in range(4):
                    if i < 3:
                        act.wait_ge(key_ps, 3 * n + i + 1)
                    else:
                        act.wait_ge(chunk_done, CHUNKS * n + KEYS_DONE)
                    A_(keys_cm[:, 4 * i:4 * i + 4, :], quad(4 + i % 2), ACT.Copy).then_inc(key_ok, 1)
                    act.wait_ge(key_ok, 4 * n + i + 1)
                for i in range(4):
                    yield 31 + 3 * max(i - 1, 0)
                    act.wait_ge(chunk_done, CHUNKS * n + Q_DONE[i])
                    A_(q_cm[:, 4 * i:4 * i + 4, :], quad(i % 2), ACT.Copy).then_inc(pq_ok, 1)
                    act.wait_ge(pq_ok, 4 * n + i + 1)
                    for m in ((), (0,), (1,), (2, 3))[i]:
                        act.wait_ge(ps_ps, 4 * n + m + 1)
                        A_(scores[:, 4 * m:4 * m + 4, :], quad(2 + m), ACT.Copy).then_inc(ps_ok, 1)
                        act.wait_ge(ps_ok, 4 * n + m + 1)
                yield 43
                act.wait_ge(bmax_ok, n + 1)
                A_(gate[:, :], gate[:, :], ACT.Exp).then_inc(gexp_ok, 1)
                act.wait_ge(gexp_ok, n + 1)

            def gather(n, q0, q1):
                for q in range(q0, q1):
                    if q == SLOTS:
                        act.wait_ge(dots_ok, n + 1)
                        A_(dots[:, :], dots[:, :], ACT.Gelu).then_inc(act_ok, 1)
                        act.wait_ge(w_ok, n + 1)
                    if q >= SLOTS and q % RING in ON_PE:
                        act.wait_ge(s_used[q % RING], USES * n + q // RING + 1)
                        A_(diag[:, ON_PE.index(q % RING), :], ident[:, :], ACT.Copy, scale=weight[:, q - SLOTS:q - SLOTS + 1])\
                            .then_inc(s_diag, 1)

            def unit_steps(n):
                if n < UNITS:
                    yield from mixing(*units[n])
                    yield from peer(*units[n])

            for _ in unit_steps(0):
                pass
            for n, layer, t in units:
                at = 0
                for step in unit_steps(n + 1):
                    if ROWS_BY[step] > at:
                        gather(n, at, ROWS_BY[step])
                        at = ROWS_BY[step]
                gather(n, at, 2 * SLOTS)

        @block.vector
        def _(dve):
            V = nc.vector
            own = Chain(s_dve, dve)
            tt, ts, stt = V.tensor_tensor, V.tensor_scalar, V.scalar_tensor_tensor
            dve.wait_ge(st_iota, 1)
            own(tt(xi[:], ti[:], pi[:], ALU.bitwise_xor))
            own.add(tt(ident[:], ti[:], pi[:], ALU.is_equal))
            own.add(tt(strict[:], ti[:], pi[:], ALU.is_gt))
            own.add(tt(incl[:], ti[:], pi[:], ALU.is_ge))
            own.add(tt(lower0[:], ti[:], pi[:], ALU.is_lt))
            own.add(V.tensor_copy(ramp[:], ti[:, 0:TOPK]))
            for k in range(LEVELS):
                own(ts(mask_i[:, k, :], xi[:], k, None, ALU.logical_shift_right))
                own(ts(level[:, k, :], mask_i[:, k, :], 1.0, None, ALU.is_equal))
            own(ts(head_ones[:], mask_i[:, 6, :], 0.0, None, ALU.is_equal))
            own(tt(lower0[:], lower0[:], level[:, 0, :], ALU.mult))
            own(tt(level[:, :, :], level[:, :, :], strict[:, :].unsqueeze(1).broadcast_to([P, LEVELS, P]), ALU.mult))
            V.tensor_copy(small_p[:, 0:1], ident[:, 0:1]).then_inc(st_masks, 1)
            dve.wait_ge(st_masks, 1)
            dve.wait_ge(s_setup, loads[0])
            dve.wait_ge(st_prow, 1)
            own(V.tensor_copy(pcol[:], bank[0][:, 0:NROWS]))
            re0, im0 = ROW["ssm_lambda_re"][0], ROW["ssm_lambda_im"][0]
            w0c = ROW["rw_decay_w0"][0]
            own.add(ts(half[:, 0:12], pcol[:, w0c:w0c + 12], 0.5, None, ALU.mult))
            for layer in range(DEPTH):
                own.add(ts(subln[:, layer:layer + 1], col("da_subln", layer, 0), 1.0 - LAM_INIT[layer], None, ALU.mult))
            lr, li, step = lrt[:, :], pcol[:, im0:im0 + 16], small[:, 16:32]
            own(ts(lr, pcol[:, re0:re0 + 16], -1e-4, None, ALU.min))
            def setup_rest():
                dve.wait_ge(s_setup_rest, 16 * REST_LOADS)
                own(tt(lam_raw4[:, :, 0, :], lam_raw4[:, :, 0, :], lam_raw4[:, :, 1, :], ALU.mult))
                own(V.tensor_reduce(small[:, 48:52], lam_raw4[:, :, 0, :], AX.X, ALU.add))
                dve.wait_ge(st_step, 1)
                own(tt(small[:, 32:48], lr, step, ALU.mult))
                own(tt(ang[:, 0, 0:16], li, step, ALU.mult))
                own(V.tensor_copy(posf[:], ti_pos[:]))
                for j in range(ROT):
                    own.add(ts(ang[:, 0, 16:32].rearrange("p (t j) -> p t j", j=ROT)[:, :, j], posf[:, :], float(INV_FREQ[j]), None, ALU.mult))
                dve.wait_ge(s_dve, own.count)
                a0, a1 = ang[:, 0, :], ang[:, 1, :]
                own(ts(a1, a0, 1.0 / (2 * math.pi), ROUNDER, ALU.mult, ALU.add))
                own(ts(a1, a1, -ROUNDER, None, ALU.add))
                own(stt(a0, a1, -TWO_PI_A, a0, ALU.mult, ALU.add))
                own(stt(a0, a1, -TWO_PI_B, a0, ALU.mult, ALU.add))
                own(stt(a0, a1, -TWO_PI_C, a0, ALU.mult, ALU.add))
                own(ts(a0, a0, PI_IN, -PI_IN, ALU.min, ALU.max))
                own(stt(a1, a0, -1.0, a0, ALU.mult, ALU.min))
                ts(a1, a1, math.pi / 2, None, ALU.add).then_inc(st_ang, 1)
                dve.wait_ge(st_ang, 1)
                dve.wait_ge(st_trig, 1)
                for layer in range(DEPTH):
                    own(tt(neg_lam[:, layer:layer + 1], small[:, 61 + 2 * layer:62 + 2 * layer], small[:, 60 + 2 * layer:61 + 2 * layer], ALU.subtract))
                    own(ts(neg_lam[:, layer:layer + 1], neg_lam[:, layer:layer + 1], -LAM_INIT[layer], None, ALU.add))
                are, aim, den, cr, ci, tmp = (s5p[:, i, :] for i in range(6))
                own.add(tt(are, mag[:], cs[:, 0:16], ALU.mult))
                own(tt(aim, mag[:], sn[:, 0:16], ALU.mult))
                own(ts(are, are, -1.0, None, ALU.add))
                own.add(tt(den, lr, lr, ALU.mult))
                own(tt(tmp, li, li, ALU.mult))
                own(tt(den, den, tmp, ALU.add))
                own(V.reciprocal(den, den))
                own.add(tt(cr, are, lr, ALU.mult))
                own(tt(tmp, aim, li, ALU.mult))
                own(tt(cr, cr, tmp, ALU.add))
                own.add(tt(cr, cr, den, ALU.mult))
                own.add(tt(ci, aim, lr, ALU.mult))
                own(tt(tmp, are, li, ALU.mult))
                own(tt(ci, ci, tmp, ALU.subtract))
                own(tt(ci, ci, den, ALU.mult))
                crb, cib = (a.unsqueeze(2).broadcast_to([P, 16, GCH]) for a in (cr, ci))
                own.add(tt(b_t[:, 0], crb, b_raw[:, 0], ALU.mult))
                own.add(tt(b_t[:, 1], cib, b_raw[:, 1], ALU.mult))
                own.add(tt(b_t[:, 2], crb, b_raw[:, 1], ALU.mult))
                own.add(tt(b_t[:, 3], cib, b_raw[:, 0], ALU.mult))
                dve.wait_ge(s_dve, own.count)
                for ri, op in ((0, ALU.subtract), (1, ALU.add)):
                    for q in range(2):
                        ps_ = slice(64 * q, 64 * q + 64)
                        dst = bd[ps_, :, ri, :].rearrange("p a (b c) -> p a b c", c=32)[:, :, :, 16 * q:16 * q + 16]
                        own.add(tt(dst, b_t[ps_, 2 * ri].rearrange("p (a b) c -> p a b c", b=4),
                                   b_t[ps_, 2 * ri + 1].rearrange("p (a b) c -> p a b c", b=4), op))
                dve.wait_ge(s_dve, own.count)
                V.tensor_copy(small_p[:, 0:1], ident[:, 0:1]).then_inc(st_bd, 1)
                dve.wait_ge(st_bd, 1)

            def input_map():
                dve.wait_ge(st_bps, 1)
                for i in range(2):
                    own.add(V.tensor_copy(bT[:, 2 * i:2 * i + 2, :, :].rearrange("p a b c -> p (a b) c"), quad(6 + i)))
                dve.wait_ge(s_dve, own.count)
                V.tensor_copy(small_p[:, 0:1], ident[:, 0:1]).then_inc(st_input, 1)
                dve.wait_ge(st_input, 1)

            def output_map():
                dve.wait_ge(st_cps, 1)
                for a in range(2 * DEPTH):
                    layer, hb_ = a // 2, a % 2
                    for ri in range(2):
                        src = quad(6 + a // 2)[:, 2 * (a % 2) + ri, :].rearrange("p (b q c) -> p b q c", q=2, c=GCH)
                        for q in range(2):
                            ps_ = slice(64 * q, 64 * q + 64)
                            own.add(ts(cT[ps_, layer, 4 * hb_:4 * hb_ + 4, ri, 16 * q:16 * q + 16], src[ps_, :, q, :],
                                       -1.0 if ri else 1.0, None, ALU.mult))
                dve.wait_ge(s_dve, own.count)
                V.tensor_copy(small_p[:, 0:1], ident[:, 0:1]).then_inc(st_done, 1)
                dve.wait_ge(st_done, 1)

            def mixing(n, layer, t):
                yield 0
                if t == 0:
                    V.memset(raw[:, 2:BLOCKS, 0:1], 0.0).then_inc(halo, 1)
                    dve.wait_ge(halo, n + 1)
                else:
                    V.tensor_copy(raw[:, 2:BLOCKS, 0:1], raw[:, 2:BLOCKS, P:P + 1]).then_inc(halo, 1)
                    dve.wait_ge(halo, n + 1)
                dve.wait_ge(x_sd, n + 1)
                own(V.reciprocal(small_m[:, 2:3], small_m[:, 1:2]))
                ts(h[:, :], x[:, t, :], small_m[:, 2:3], None, ALU.mult).then_inc(h_ok, 1)
                dve.wait_ge(h_ok, n + 1)
                yield 1
                dve.wait_ge(hT_ps, 2 * n + 2)
                for k in range(4, 8):
                    ins = ts(h_cm[:, k, :], quad(1)[:, k - 4, :], col("norm_mix", layer, k), None, ALU.mult)
                    if k < 7:
                        own.add(ins)
                ins.then_inc(hT_v, 1)
                dve.wait_ge(hT_v, n + 1)
                yield 2
                if n == 0:
                    setup_rest()
                dve.wait_ge(raw_ok, 3 * n + 3)
                own(tt(cc[:, :, :], raw[:, 2:BLOCKS, 0:P], raw[:, 2:BLOCKS, 1:P + 1], ALU.subtract))
                for b in range(7):
                    ins = stt(cc[:, b, :], cc[:, b, :], col("rw_mu", layer, b), raw[:, 2 + b, 1:P + 1], ALU.mult, ALU.add)
                    if b < 6:
                        own.add(ins)
                dve.wait_ge(s_dve, own.count)
                ins.then_inc(cc_ok, 1)
                dve.wait_ge(cc_ok, n + 1)
                yield 3
                dve.wait_ge(qk_sq, n + 1)
                V.tensor_reduce(small_m[:, 16:32], sqs[:, :, :].rearrange("p a (b d) -> p (a b) d", d=HD), AX.X, ALU.add).then_inc(qk_ss, 1)
                dve.wait_ge(qk_ss, n + 1)
                yield 4
                dve.wait_ge(qk_sd, n + 1)
                own(V.reciprocal(small_m[:, 32:48], small_m[:, 32:48]))
                for i in range(2):
                    r8 = small_m[:, 32 + 8 * i:40 + 8 * i].unsqueeze(2).broadcast_to([P, 8, HD])
                    own.add(tt(qk[:, i, :].rearrange("p (b d) -> p b d", d=HD), bank[i][:, :].rearrange("p (b d) -> p b d", d=HD), r8, ALU.mult))
                dve.wait_ge(s_dve, own.count)
                dve.wait_ge(s_gain, 48 * (layer + 1))
                own(tt(qk[:, :, :], qk[:, :, :], gain_qk[:, :, :], ALU.mult))
                r = qk[:, :, :].rearrange("p a (b d) -> p (a b) d", d=HD)
                r1, r2 = r[:, :, 0:ROT], r[:, :, ROT:2 * ROT]
                c8, s8 = (a[:, 16 + ROT * t:16 + ROT * t + ROT].unsqueeze(1).broadcast_to([P, 16, ROT]) for a in (cs, sn))
                own.add(tt(qk_tmp[:, 0], r1, c8, ALU.mult))
                own.add(tt(qk_tmp[:, 1], r2, s8, ALU.mult))
                own.add(tt(qk_tmp[:, 2], r2, c8, ALU.mult))
                own.add(tt(qk_tmp[:, 3], r1, s8, ALU.mult))
                dve.wait_ge(s_dve, own.count)
                own.add(tt(r1, qk_tmp[:, 0], qk_tmp[:, 1], ALU.subtract))
                dve.wait_ge(s_dve, own.count)
                tt(r2, qk_tmp[:, 2], qk_tmp[:, 3], ALU.add).then_inc(qk_ok, 1)
                dve.wait_ge(qk_ok, n + 1)
                yield 5
                dve.wait_ge(lora_a, n + 1)
                ts(rw["lora"][64:128, 0, :], rw["lora"][64:128, 0, :], 0.5, 0.5, ALU.mult, ALU.add).then_inc(lora_in, 1)
                dve.wait_ge(lora_in, n + 1)
                rr, kk_, vv = cc[:, 0:2, :], cc[:, 2:4, :], cc[:, 4:6, :]
                for b in range(2):
                    own.add(ts(rw["kk"][:, b, :], kk_[:, b, :], col("rw_k_k", layer, b), None, ALU.mult))
                dve.wait_ge(s_dve, own.count)
                tt(rw["k2"][:, :, :], rw["kk"][:, :, :], rw["kk"][:, :, :], ALU.mult).then_inc(kk_sq, 1)
                dve.wait_ge(kk_sq, n + 1)
                yield 6
                dve.wait_ge(lora_ok, n + 1)
                own.add(ts(rw["a"][:, :, :], rw["a"][:, :, :], 0.5, 0.5, ALU.mult, ALU.add))
                own(ts(rw["ep"][:, :, :], rw["ep"][:, :, :], -0.5 * C_DECAY, -0.5 * C_DECAY, ALU.mult, ALU.add))
                for b in range(2):
                    own.add(V.tensor_tensor_scan(cum[:, b, 1:P + 1], ones[:, :], rw["ep"][:, b, :], 0.0, ALU.mult, ALU.add))
                dve.wait_ge(s_dve, own.count)
                ts(small_m[:, 4:6], cum[:, :, CHUNK], -1.0, None, ALU.mult).then_inc(cum_ok, 1)
                dve.wait_ge(cum_ok, n + 1)
                yield 7
                dve.wait_ge(qkT_ps, 2 * n + 2)
                V.tensor_copy(kT[:, :, P * t:P * t + P], quad(1)).then_inc(kT_ok, 1)
                dve.wait_ge(kT_ok, n + 1)
                yield 8
                dve.wait_ge(kk_sd, n + 1)
                own(ts(rw["rk"][:, :, :], rw["rk"][:, :, :], 1e-12, None, ALU.max))
                own(V.reciprocal(rw["rk"][:, :, :], rw["rk"][:, :, :]))
                own(tt(rw["kk"][:, :, :], rw["kk"][:, :, :], rw["rk"][:, :, :], ALU.mult))
                dve.wait_ge(exps, n + 1)
                own.add(stt(rw["al"][:, :, :], rw["kk"][:, :, :], -1.0, rw["eq"][:, :, :], ALU.mult, ALU.mult))
                own(tt(rw["bm"][:, :, :], rw["kk"][:, :, :], rw["a"][:, :, :], ALU.mult))
                own.add(tt(rw["bm"][:, :, :], rw["bm"][:, :, :], rw["em"][:, :, :], ALU.mult))
                for b in range(2):
                    own.add(ts(rw["k2"][:, b, :], rw["a"][:, b, :], -1.0, col("rw_k_a", layer, b), ALU.add, ALU.mult))
                dve.wait_ge(s_dve, own.count)
                own(stt(rw["k2"][:, :, :], rw["k2"][:, :, :], 1.0, kk_, ALU.add, ALU.mult))
                own.add(tt(rw["km"][:, :, :], rw["k2"][:, :, :], rw["em"][:, :, :], ALU.mult))
                own.add(tt(rw["rp"][:, :, :], rr, rw["ep"][:, :, :], ALU.mult))
                own(tt(rw["k2"][:, :, :], rw["k2"][:, :, :], rr, ALU.mult))
                for b in range(2):
                    own.add(ts(rw["rk"][:, b, :], rw["k2"][:, b, :], col("rw_r_k", layer, b), None, ALU.mult))
                if t == 0:
                    own(V.memset(state[:], 0.0))
                for b in range(2):
                    own.add(ts(state0[:, b, :], state[:, b, :], small_m[:, 6 + b:7 + b], None, ALU.mult))
                own.add(V.tensor_copy(small_m[:, 10:12], rw["ep"][:, :, P - 1]))
                dve.wait_ge(s_dve, own.count)
                V.tensor_copy(small_m[:, 12:13], eps[:, 0:1]).then_inc(abkr, 1)
                dve.wait_ge(abkr, n + 1)
                yield 9
                if n == 0:
                    input_map()
                dve.wait_ge(mats, n + 1)
                for par in range(2):
                    hs = slice(2 * par, 2 * par + 2)

                    def masked_by(dst, src, mask):
                        own.add(tt(dst[:, hs, :], src, mask.unsqueeze(1).broadcast_to([P, 2, P]), ALU.mult))

                    masked_by(mT, quad(0 + par)[:, 0:2, :], strict[:, :])
                    masked_by(inv, quad(0 + par)[:, 2:4, :], lower0[:, :])
                    masked_by(nT, quad(2 + par)[:, 0:2, :], strict[:, :])
                    masked_by(rbT, quad(2 + par)[:, 2:4, :], incl[:, :])
                    masked_by(rkT, quad(4 + par)[:, 0:2, :], incl[:, :])
                dve.wait_ge(s_dve, own.count)
                ib = ident[:, :].unsqueeze(1).broadcast_to([P, HEADS, P])
                own.add(tt(inv[:, :, :], inv[:, :, :], ib, ALU.add))
                own(tt(invT[:, :, :], mT[:, :, :], level[:, 0:1, :].broadcast_to([P, HEADS, P]), ALU.mult))
                tt(invT[:, :, :], invT[:, :, :], ib, ALU.add).then_inc(masked, 1)
                dve.wait_ge(masked, n + 1)

                def joined(k):
                    return tt(ms[k % 2][:, :, :], mT[:, :, :], level[:, k:k + 1, :].broadcast_to([P, HEADS, P]), ALU.mult)

                def phase_doubling(k):
                    if k == 0:
                        own.add(V.tensor_copy(e_cos[:, :, 0], cs[:, SB * layer:SB * layer + SB]))
                        own(V.tensor_copy(e_sin[:, :, 0], sn[:, SB * layer:SB * layer + SB]))
                    m = 1 << k
                    cm, sm = (e[:, :, m - 1:m].broadcast_to([P, SB, m]) for e in (e_cos, e_sin))
                    own.add(tt(dbl[:, :, 0:m], e_cos[:, :, 0:m], cm, ALU.mult))
                    own.add(tt(e_cos[:, :, m:2 * m], e_sin[:, :, 0:m], sm, ALU.mult))
                    dve.wait_ge(s_dve, own.count)
                    own.add(tt(e_cos[:, :, m:2 * m], dbl[:, :, 0:m], e_cos[:, :, m:2 * m], ALU.subtract))
                    dve.wait_ge(s_dve, own.count)
                    own.add(tt(dbl[:, :, 0:m], e_cos[:, :, 0:m], sm, ALU.mult))
                    own.add(tt(e_sin[:, :, m:2 * m], e_sin[:, :, 0:m], cm, ALU.mult))
                    dve.wait_ge(s_dve, own.count)
                    own(tt(e_sin[:, :, m:2 * m], dbl[:, :, 0:m], e_sin[:, :, m:2 * m], ALU.add))

                joined(1).then_inc(ms_ok, 1)
                dve.wait_ge(ms_ok, NL * n + 1)
                for k in range(1, LEVELS):
                    if k < NL:
                        joined(k + 1).then_inc(ms_ok, 1)
                        dve.wait_ge(ms_ok, NL * n + k + 1)
                    if t == 0:
                        if k == 1:
                            phase_doubling(0)
                        phase_doubling(k)
                    yield 9 + k
                    dve.wait_ge(up_ps, NL * n + k)
                    if k < LEVELS - 1:
                        own(tt(inv[:, :, :], inv[:, :, :], quad(1), ALU.add))
                    tt(invT[:, :, :], invT[:, :, :], quad(2), ALU.add).then_inc(up_ok, 1)
                    dve.wait_ge(up_ok, NL * n + k)
                yield 16
                if n == 0:
                    output_map()
                dve.wait_ge(rhs_ps, n + 1)
                for par in range(2):
                    ins = V.tensor_copy(rhs[:, 2 * par:2 * par + 2, :], bank[par][:, 0:P].rearrange("p (a t) -> p a t", t=HD))
                    if par == 0:
                        own.add(ins)
                dve.wait_ge(s_dve, own.count)
                ins.then_inc(rhs_ok, 1)
                dve.wait_ge(rhs_ok, n + 1)
                yield 17
                dve.wait_ge(y_ps, n + 1)
                for par in range(2):
                    ps_ = slice(64 * par, 64 * par + 64)
                    own.add(V.tensor_copy(rw["y"][ps_, :, :], quad(3 + par)[ps_, 0:2, :]))
                own(tt(state[:, :, :], state0[:, :, :], bank[5][:, 0:P].rearrange("p (a t) -> p a t", t=HD), ALU.add))
                for b in range(2):
                    own.add(ts(state[:, b, :], state[:, b, :], small_m[:, 10 + b:11 + b], None, ALU.mult))
                dve.wait_ge(s_dve, own.count)
                V.tensor_copy(small_m[:, 12:13], eps[:, 0:1]).then_inc(y_ok, 1)
                dve.wait_ge(y_ok, n + 1)
                yield 18
                dve.wait_ge(mean_ps, n + 1)
                own(stt(rw["y"][:, :, :], quad(0)[:, 0:2, :], -1.0 / HD, rw["y"][:, :, :], ALU.mult, ALU.add))
                tt(rw["kk"][:, :, :], rw["y"][:, :, :], rw["y"][:, :, :], ALU.mult).then_inc(dev_ok, 1)
                dve.wait_ge(dev_ok, n + 1)
                own(tt(rw["k2"][:, :, :], quad(2)[:, 0:2, :], vv, ALU.mult))
                yield 19
                dve.wait_ge(var_sd, n + 1)
                own(V.reciprocal(rw["ep"][:, :, :], rw["ep"][:, :, :]))
                own(tt(rw["y"][:, :, :], rw["y"][:, :, :], rw["ep"][:, :, :], ALU.mult))
                for b in range(2):
                    own.add(ts(rw["y"][:, b, :], rw["y"][:, b, :], col("rw_ln_w", layer, b), col("rw_ln_b", layer, b), ALU.mult, ALU.add))
                dve.wait_ge(s_dve, own.count)
                own(tt(rw["y"][:, :, :], rw["y"][:, :, :], rw["k2"][:, :, :], ALU.add))
                tt(mixed[:, 6:8, :], rw["y"][:, :, :], rw["g"][:, :, :], ALU.mult).then_inc(mix_r, 1)
                dve.wait_ge(mix_r, n + 1)
                for hf in range(2):
                    yield 20 + hf
                    dve.wait_ge(bu_ps, 2 * n + hf + 1)
                    bs = slice(4 * hf, 4 * hf + 4)
                    ec, es = (e[:, 4 * hf:4 * hf + 4, :] for e in (e_cos, e_sin))
                    re_, im_ = quad(2 * hf), quad(2 * hf + 1)
                    own.add(tt(zin[0][:, bs, :], re_, ec, ALU.mult))
                    own.add(tt(z[0][:, bs, :], im_, es, ALU.mult))
                    own.add(tt(zin[1][:, bs, :], im_, ec, ALU.mult))
                    own.add(tt(z[1][:, bs, :], re_, es, ALU.mult))
                    dve.wait_ge(s_dve, own.count)
                    own.add(tt(zin[0][:, bs, :], zin[0][:, bs, :], z[0][:, bs, :], ALU.add))
                    dve.wait_ge(s_dve, own.count)
                    tt(zin[1][:, bs, :], zin[1][:, bs, :], z[1][:, bs, :], ALU.subtract).then_inc(z_ok, 1)
                    dve.wait_ge(z_ok, 2 * n + hf + 1)
                yield 22
                for b in range(SB):
                    m = mag[:, SB * layer + b:SB * layer + b + 1].broadcast_to([P, P])
                    for ri in range(2):
                        first = carry[:, ri, b:b + 1] if t else 0.0
                        own.add(V.tensor_tensor_scan(z[ri][:, b, :], m, zin[ri][:, b, :], first, ALU.mult, ALU.add))
                dve.wait_ge(s_dve, own.count)
                ec, es = (e[:, :, :] for e in (e_cos, e_sin))
                own.add(tt(zin[0][:, :, :], ec, z[0][:, :, :], ALU.mult))
                own.add(tt(zin[1][:, :, :], es, z[1][:, :, :], ALU.mult))
                dve.wait_ge(s_dve, own.count)
                own.add(tt(zin[0][:, :, :], zin[0][:, :, :], zin[1][:, :, :], ALU.subtract))
                dve.wait_ge(s_dve, own.count)
                own.add(tt(zin[1][:, :, :], es, z[0][:, :, :], ALU.mult))
                own.add(tt(z[1][:, :, :], ec, z[1][:, :, :], ALU.mult))
                dve.wait_ge(s_dve, own.count)
                own(tt(zin[1][:, :, :], zin[1][:, :, :], z[1][:, :, :], ALU.add))
                own.add(V.tensor_copy(carry[:, 0, :], zin[0][:, :, P - 1]))
                V.tensor_copy(carry[:, 1, :], zin[1][:, :, P - 1]).then_inc(xs_ok, 1)
                dve.wait_ge(xs_ok, n + 1)
                yield 23
                dve.wait_ge(sy_ps, n + 1)
                for hf in range(2):
                    ins = stt(glu_t[:, hf, :], raw[:, hf, 1:P + 1], col("ssm_d", layer, hf), quad(4)[:, hf, :], ALU.mult, ALU.add)
                    if hf == 0:
                        own.add(ins)
                dve.wait_ge(s_dve, own.count)
                ins.then_inc(sy_ok, 1)
                dve.wait_ge(sy_ok, n + 1)
                yield 24
                dve.wait_ge(glu_th, n + 1)
                own(ts(glu_t[:, :, :], glu_t[:, :, :], 0.5, 0.5, ALU.mult, ALU.add))
                own(tt(glu_o[:, :, :], glu_t[:, :, :], yg[:, :, :], ALU.mult))
                tt(yg[:, :, :], glu_o[:, :, :], glu_o[:, :, :], ALU.mult).then_inc(glu_sq, 1)
                dve.wait_ge(glu_sq, n + 1)
                yield 25
                dve.wait_ge(gss_sd, n + 1)
                own(V.reciprocal(glu_t[:, 0, :], glu_t[:, 0, :]))
                for hf in range(2):
                    ins = stt(mixed[:, 4 + hf, :], glu_o[:, hf, :], col("ssm_out_norm", layer, hf), glu_t[:, 0, :], ALU.mult, ALU.mult)
                    if hf == 0:
                        own.add(ins)
                dve.wait_ge(s_dve, own.count)
                ins.then_inc(mix_s, 1)
                dve.wait_ge(mix_s, n + 1)
                yield 26
                dve.wait_ge(sc_ps, n + 1)
                kv = P * (t + 1)
                nb = 2 * (t + 1)
                per = 8 // nb
                for i in range(nb):
                    own.add(V.memset(bank[i][0:CHUNK, :].rearrange("p (a k) -> p a k", k=kv)[:, :, kv - CHUNK:kv], -1e30))
                dve.wait_ge(s_dve, own.count)
                for i in range(nb):
                    own.add(V.tensor_reduce(small_a[:, per * i:per * i + per], bank[i][:, :].rearrange("p (a k) -> p a k", k=kv), AX.X, ALU.max))
                dve.wait_ge(s_dve, own.count)
                ts(small_a[:, 8:16], small_a[:, 0:8], -SCALE, None, ALU.mult).then_inc(max_ok, 1)
                dve.wait_ge(max_ok, n + 1)
                yield 27
                dve.wait_ge(exp_ok, n + 1)
                own(V.reciprocal(small_a[:, 16:24], small_a[:, 16:24]))
                own(ts(small_a[:, 20:24], small_a[:, 20:24], neg_lam[:, layer:layer + 1], None, ALU.mult))
                for hd in range(HEADS):
                    own.add(ts(probs[:, 0, hd, 0:kv], probs[:, 0, hd, 0:kv], small_a[:, 16 + hd:17 + hd], None, ALU.mult))
                dve.wait_ge(s_dve, own.count)
                for hd in range(HEADS):
                    ins = stt(probs[:, 0, hd, 0:kv], probs[:, 1, hd, 0:kv], small_a[:, 20 + hd:21 + hd], probs[:, 0, hd, 0:kv], ALU.mult, ALU.add)
                    if hd < HEADS - 1:
                        own.add(ins)
                dve.wait_ge(s_dve, own.count)
                ins.then_inc(comb_ok, 1)
                dve.wait_ge(comb_ok, n + 1)
                yield 28
                dve.wait_ge(oss_sd, n + 1)
                own(V.reciprocal(o_rs[:, :], o_rs[:, :]))
                stt(mixed[:, 0:4, :].rearrange("p a t -> p (a t)"), bank[2][:, :], subln[:, layer:layer + 1], o_rs[:, :], ALU.mult, ALU.mult).then_inc(mix_d, 1)
                dve.wait_ge(mix_d, n + 1)
                yield 29
                for i in range(2):
                    dve.wait_ge(chunk_done, CHUNKS * n + OUT_DONE[i])
                    ins = tt(x[:, t, 512 * i:512 * i + 512], x[:, t, 512 * i:512 * i + 512], bank[i][:, :], ALU.add)
                    if i == 0:
                        own.add(ins)
                dve.wait_ge(s_dve, own.count)
                ins.then_inc(x_mid, 1)
                dve.wait_ge(x_mid, n + 1)

            def peer(n, layer, t):
                yield 30
                dve.wait_ge(f_sd, n + 1)
                own(V.reciprocal(small_p[:, 2:3], small_p[:, 1:2]))
                stt(hb[:, :], x[:, t, :], small_p[:, 2:3], gain_ffn[:, :], ALU.mult, ALU.mult).then_inc(f_h, 1)
                dve.wait_ge(f_h, n + 1)
                yield 31
                dve.wait_ge(fT_ps, 2 * n + 2)
                V.tensor_copy(hb_cm[:, 4:8, :], quad(3)).then_inc(fT_v, 1)
                dve.wait_ge(fT_v, n + 1)
                for i in range(4):
                    blocks, heads = range(4 * i, 4 * i + 4), range(2 * i, 2 * i + 2)
                    yield 32 + 3 * i
                    dve.wait_ge(ps_ok, 4 * n + i + 1)
                    for b in blocks:
                        own.add(V.max(tops[:, b, 0:8], scores[:, b, :]))
                    dve.wait_ge(s_dve, own.count)
                    for b in blocks:
                        own.add(V.max_index(topi[:, b, 0:8], tops[:, b, 0:8], scores[:, b, :]))
                    dve.wait_ge(s_dve, own.count)
                    for b in blocks:
                        own.add(V.match_replace(scores[:, b, :], tops[:, b, 0:8], scores[:, b, :], -3e38))
                    dve.wait_ge(s_dve, own.count)
                    yield 33 + 3 * i
                    for b in blocks:
                        own.add(V.max(tops[:, b, 8:16], scores[:, b, :]))
                    dve.wait_ge(s_dve, own.count)
                    for b in blocks:
                        own.add(V.max_index(topi[:, b, 8:16], tops[:, b, 8:16], scores[:, b, :]))
                    dve.wait_ge(s_dve, own.count)
                    for hd in heads:
                        first = tops[:, 2 * hd, :].unsqueeze(2).broadcast_to([P, TOPK, TOPK])
                        second = tops[:, 2 * hd + 1, :].unsqueeze(1).broadcast_to([P, TOPK, TOPK])
                        own.add(tt(cand[:, hd, :].rearrange("p (a b) -> p a b", b=TOPK), first, second, ALU.add))
                    dve.wait_ge(s_dve, own.count)
                    yield 34 + 3 * i
                    for hd in heads:
                        own.add(V.max(best[:, hd, 0:8], cand[:, hd, :]))
                    dve.wait_ge(s_dve, own.count)
                    for hd in heads:
                        own.add(V.max_index(bpos[:, hd, 0:8], best[:, hd, 0:8], cand[:, hd, :]))
                    dve.wait_ge(s_dve, own.count)
                    for hd in heads:
                        own.add(V.match_replace(cand[:, hd, :], best[:, hd, 0:8], cand[:, hd, :], -3e38))
                    dve.wait_ge(s_dve, own.count)
                    for hd in heads:
                        own.add(V.max(best[:, hd, 8:16], cand[:, hd, :]))
                    dve.wait_ge(s_dve, own.count)
                    for hd in heads:
                        own.add(V.max_index(bpos[:, hd, 8:16], best[:, hd, 8:16], cand[:, hd, :]))
                    dve.wait_ge(s_dve, own.count)
                yield 43
                g3 = gate[:, :].rearrange("p (a b) -> p a b", b=TOPK)
                tt(g3, best[:, :, :], best[:, :, 0:1].broadcast_to([P, PEER_HEADS, TOPK]), ALU.subtract).then_inc(bmax_ok, 1)
                dve.wait_ge(bmax_ok, n + 1)
                own.add(V.tensor_copy(topf[:, :, :], topi[:, :, :]))
                own.add(ts(bhi[:, :, :], bpos[:, :, :], 4, None, ALU.logical_shift_right))
                dve.wait_ge(s_dve, own.count)
                own.add(V.tensor_copy(fhi[:, :], bhi[:, :, :].rearrange("p a b -> p (a b)")))
                own.add(ts(bpos[:, :, :], bpos[:, :, :], 15, None, ALU.bitwise_and))
                dve.wait_ge(s_dve, own.count)
                own(V.tensor_copy(flo[:, :], bpos[:, :, :].rearrange("p a b -> p (a b)")))
                for m, f in ((0, fhi), (1, flo)):
                    yield 44 + m
                    own(tt(picked[:, :, :], f[:, :].unsqueeze(2).broadcast_to([P, SLOTS, TOPK]),
                           ramp[:, :].unsqueeze(1).broadcast_to([P, SLOTS, TOPK]), ALU.is_equal))
                    ids = topf[:, :, :].rearrange("p (a m) c -> p a m c", m=2)[:, :, m:m + 1, :].broadcast_to([P, PEER_HEADS, TOPK, TOPK])
                    p4 = picked[:, :, :].rearrange("p (a b) c -> p a b c", b=TOPK)
                    own(tt(p4, p4, ids, ALU.mult))
                    own(V.tensor_reduce(f[:, :], picked[:, :, :], AX.X, ALU.add))
                yield 46
                own(ts(fhi[:, :], fhi[:, :], float(NKEYS), float(layer * N_EXPERTS), ALU.mult, ALU.add))
                tt(expert[:, n % 2, :], fhi[:, :], flo[:, :], ALU.add).then_inc(ids_ok, 1)
                dve.wait_ge(ids_ok, n + 1)
                yield 47
                dve.wait_ge(gexp_ok, n + 1)
                own(V.tensor_reduce(small_p[:, 8:16], g3, AX.X, ALU.add))
                own(V.reciprocal(small_p[:, 8:16], small_p[:, 8:16]))
                own(tt(g3, g3, small_p[:, 8:16].unsqueeze(2).broadcast_to([P, PEER_HEADS, TOPK]), ALU.mult))

            def gather(n, q0, q1):
                for q in range(q0, q1):
                    j, use = q % RING, USES * n + q // RING
                    if q == SLOTS:
                        for k in range(RING):
                            dve.wait_ge(s_used[k], use + 1)
                        own(V.memset(y_rows[:, :], 0.0))
                        V.tensor_copy(small_p[:, 4:5], eps[:, 0:1]).then_inc(dots_ok, 1)
                        dve.wait_ge(dots_ok, n + 1)
                        dve.wait_ge(act_ok, n + 1)
                        tt(weight[:, :], gate[:, :], dots[:, :], ALU.mult).then_inc(w_ok, 1)
                        dve.wait_ge(w_ok, n + 1)
                    if q < SLOTS:
                        dve.wait_ge(s_row[j], 16 * (use + 1))
                        stt(rows[j], rows[j], 1.0, hb[:, :], ALU.mult, ALU.mult, accum_out=dots[:, q:q + 1]).then_inc(s_used[j], 1)
                    elif j in ON_DVE:
                        dve.wait_ge(s_row[j], 16 * (use + 1))
                        before = ON_DVE[ON_DVE.index(j) - 1]
                        dve.wait_ge(s_used[before], use + (2 if before < j else 1))
                        stt(y_rows[:, :], rows[j], weight[:, q - SLOTS:q - SLOTS + 1], y_rows[:, :], ALU.mult, ALU.add)\
                            .then_inc(s_used[j], 1)

            def add_rows(n, t):
                dve.wait_ge(s_used[ON_DVE[-1]], 1 + USES * (n + 1))
                own(tt(x[:, t, :], x[:, t, :], y_rows[:, :], ALU.add))
                dve.wait_ge(y_done, n + 1)
                own.add(tt(x[:, t, 0:512], x[:, t, 0:512], bank[6][:, :], ALU.add))
                tt(x[:, t, 512:1024], x[:, t, 512:1024], bank[7][:, :], ALU.add).then_inc(ffn_done, 1)
                dve.wait_ge(ffn_done, n + 1)

            def unit_steps(n):
                if n < UNITS:
                    yield from mixing(*units[n])
                    yield from peer(*units[n])

            for _ in unit_steps(0):
                pass
            for n, layer, t in units:
                at = 0
                for step in unit_steps(n + 1):
                    if ROWS_BY[step] > at:
                        gather(n, at, ROWS_BY[step])
                        at = ROWS_BY[step]
                gather(n, at, 2 * SLOTS)
                add_rows(n, t)

        @block.tensor
        def _(pe):
            mm, tr = nc.tensor.matmul, nc.tensor.transpose
            pe.wait_ge(st_masks, 1)
            pe.wait_ge(s_setup, loads[0])
            tr(bank[0][:, 0:NROWS], prow[:, :], ident[0:NROWS, 0:NROWS]).then_inc(st_prow, 1)
            nothing = level[:, 0:4, :].rearrange("p a t -> p (a t)")
            g = [0]

            def chunk():
                i = g[0]
                pe.wait_ge(s_w[i % WRING], 16 * (i // WRING + 1))
                return wring[:, i % WRING]

            def chunk_used(last):
                last.then_inc(chunk_done, 1)
                g[0] += 1

            def mixing(n, layer, t):
                yield 0
                pe.wait_ge(h_ok, n + 1)
                if n:
                    pe.wait_ge(ps_ok, 4 * n)
                for k in range(KD):
                    last = tr(quad(k // 4)[:, k % 4, :], h[:, P * k:P * k + P], ident[:, :])
                    if k % 4 == 3:
                        last.then_inc(hT_ps, 1)
                pe.wait_ge(hT_a, n + 1)
                yield 1
                pe.wait_ge(hT_v, n + 1)
                b = 0
                for c0, width in BC_CHUNKS:
                    w = chunk()
                    for j in range(width // P):
                        for k in range(KD):
                            last = mm(quad(2 + b // 4)[:, b % 4, :], w[:, k, P * j:P * j + P], h_cm[:, k, :], start=k == 0, stop=k == KD - 1)
                        b += 1
                    chunk_used(last)
                for c, (c0, width) in enumerate(DA_CHUNKS):
                    w = chunk()
                    dst = bank[(0, 1, 5)[c // 2]][:, CW * (c % 2):CW * (c % 2) + CW]
                    for k in range(KD):
                        last = mm(dst, h_cm[:, k, :], w[:, k, :], start=k == 0, stop=k == KD - 1)
                    chunk_used(last)
                if n == 0:
                    pe.wait_ge(st_bd, 1)
                    for i in range(4):
                        for ri in range(2):
                            last = tr(quad(6 + i // 2)[:, 2 * (i % 2) + ri, :], bd[:, i, ri, :], ident[:, :])
                    last.then_inc(st_bps, 1)
                pe.wait_ge(raw_ok, 3 * n + 3)
                yield 5
                pe.wait_ge(lora_in, n + 1)
                for b in range(2):
                    bs = slice(P * b, P * b + P)
                    mm(bank[2][:, bs], lora_w[0:32, layer, bs], rw["lora"][0:32, 0, :], start=True, stop=True)
                    mm(bank[3][:, bs], lora_w[32:64, layer, bs], rw["lora"][32:64, 0, :], start=True, stop=True)
                    last = mm(bank[4][:, bs], lora_w[64:128, layer, bs], rw["lora"][64:128, 0, :], start=True, stop=True)
                last.then_inc(lora_ps, 1)
                pe.wait_ge(kk_sq, n + 1)
                pe.wait_ge(v_ok, n + 1)
                mm(bank[5][:, 0:256], head_ones[:, :], rw["k2"][:, :, :].rearrange("p b t -> p (b t)"), start=True, stop=True).then_inc(kk_ps, 1)
                pe.wait_ge(qk_ok, n + 1)
                for i in range(2):
                    for hd in range(HEADS):
                        last = tr(quad(i)[:, hd, :], qk[:, i, P * hd:P * hd + P], ident[:, :])
                    last.then_inc(qkT_ps, 1)
                yield 8
                pe.wait_ge(abkr, n + 1)
                pe.wait_ge(qT_ok, n + 1)
                pe.wait_ge(kT_ok, n + 1)
                pe.wait_ge(lora_ok, n + 1)
                pe.wait_ge(kk_sd, n + 1)
                pairs = ((0, 0, "bm", "al"), (0, 2, "al", "bm"), (2, 0, "km", "al"), (2, 2, "bm", "rp"), (4, 0, "km", "rp"))
                for b0, at, left, right in pairs:
                    for par in range(2):
                        ps_ = slice(64 * par, 64 * par + 64)
                        for pr in range(2):
                            last = mm(quad(b0 + par)[:, at + pr, :], rw[left][ps_, pr, :], rw[right][ps_, pr, :], start=True, stop=True)
                last.then_inc(mats, 1)
                yield 9
                pe.wait_ge(masked, n + 1)
                for i, src in enumerate((cc[:, 4:6, :], rw["bm"], rw["km"])):
                    for b in range(2):
                        last = tr(quad(4 + i // 2)[:, 2 * (i % 2) + b, :], src[:, b, :], ident[:, :])
                last.then_inc(tr_ps, 1)
                for k in range(1, LEVELS):
                    pe.wait_ge(ms_ok, NL * n + k)
                    if k > 1:
                        yield 8 + k
                        pe.wait_ge(up_ok, NL * n + k - 1)
                    for i in range(HEADS):
                        last = mm(quad(0)[:, i, :], ms[k % 2][:, i, :], inv[:, i, :], start=True, stop=True)
                    last.then_inc(pr_ps, 1)
                    yield 8 + k
                    pe.wait_ge(pr_ok, NL * n + k)
                    for i in range(HEADS):
                        if k < LEVELS - 1:
                            mm(quad(1)[:, i, :], invT[:, i, :], prod[:, i, :], start=True, stop=True)
                        last = mm(quad(2)[:, i, :], prod[:, i, :], invT[:, i, :], start=True, stop=True)
                    last.then_inc(up_ps, 1)
                yield 15
                pe.wait_ge(up_ok, NL * n + NL)
                pe.wait_ge(tok_ok, n + 1)
                if n == 0:
                    pe.wait_ge(st_input, 1)
                    for i in range(4):
                        for ri in range(2):
                            last = tr(quad(6 + i // 2)[:, 2 * (i % 2) + ri, :], c_raw[:, ri, i, :], ident[:, :])
                    last.then_inc(st_cps, 1)
                heads = [(2 * par + pr, par, pr, slice(64 * par, 64 * par + 64)) for par in range(2) for pr in range(2)]
                for i, par, pr, ps_ in heads:
                    dst = bank[par][:, HD * pr:HD * pr + HD]
                    mm(dst, rw["al"][ps_, pr, :], state0[ps_, pr, :], start=True, stop=False)
                    last = mm(dst, nT[:, i, :], tok[:, 0, pr, ps_], start=False, stop=True)
                last.then_inc(rhs_ps, 1)
                yield 16
                pe.wait_ge(rhs_ok, n + 1)
                for i, par, pr, ps_ in heads:
                    last = mm(bank[2][:, HD * i:HD * i + HD], invT[:, i, :], rhs[:, i, :], start=True, stop=True)
                last.then_inc(sa_ps, 1)
                pe.wait_ge(sa_ok, n + 1)
                for i, par, pr, ps_ in heads:
                    dst = quad(3 + par)[ps_, pr, :]
                    mm(dst, state0[ps_, pr, :], rw["rp"][ps_, pr, :], start=True, stop=False)
                    mm(dst, sa[:, i, :], rbT[:, i, :], start=False, stop=False)
                    mm(dst, tok[:, 0, pr, ps_], rkT[:, i, :], start=False, stop=True)
                    dst = bank[5][ps_, HD * pr:HD * pr + HD]
                    mm(dst, tok[:, 1, pr, ps_], sa[:, i, :], start=True, stop=False)
                    last = mm(dst, tok[:, 2, pr, ps_], tok[:, 0, pr, ps_], start=False, stop=True)
                last.then_inc(y_ps, 1)
                yield 17
                pe.wait_ge(y_ok, n + 1)
                mm(bank[2][:, 0:256], head_ones[:, :], rw["rk"][:, :, :].rearrange("p b t -> p (b t)"), start=True, stop=True)
                mm(bank[0][:, 0:256], head_ones[:, :], rw["y"][:, :, :].rearrange("p b t -> p (b t)"), start=True, stop=True).then_inc(mean_ps, 1)
                yield 18
                pe.wait_ge(dev_ok, n + 1)
                mm(bank[1][:, 0:256], head_ones[:, :], rw["kk"][:, :, :].rearrange("p b t -> p (b t)"), start=True, stop=True).then_inc(var_ps, 1)
                pe.wait_ge(u4_ok, n + 1)
                yield 19
                pe.wait_ge(mix_r, n + 1)
                for hf in range(2):
                    for b in range(4):
                        for ri in range(2):
                            last = mm(quad(2 * hf + ri)[:, b, :], bT[:, 2 * layer + hf, ri, :], u4[:, b, hf, :], start=True, stop=True)
                    last.then_inc(bu_ps, 1)
                yield 22
                pe.wait_ge(xs_ok, n + 1)
                for hf in range(2):
                    for b in range(4):
                        for ri in range(2):
                            last = mm(quad(4)[32 * b:32 * b + 32, hf, :], cT[:, layer, 4 * hf + b, ri, :], zin[ri][:, 4 * hf + b, :],
                                      start=ri == 0, stop=ri == 1)
                last.then_inc(sy_ps, 1)
                yield 23
                pe.wait_ge(gelu_ok, n + 1)
                for o in range(2):
                    for k in range(2):
                        last = mm(quad(3)[:, o, :], glu_w[:, layer, k, P * o:P * o + P], yg[:, k, :], start=k == 0, stop=k == 1)
                last.then_inc(glu_ps, 1)
                yield 24
                pe.wait_ge(glu_sq, n + 1)
                for k in range(2):
                    last = mm(bank[4][:, 0:P], ones[:, :], yg[:, k, :], start=k == 0, stop=k == 1)
                last.then_inc(gss_ps, 1)
                yield 25
                pe.wait_ge(mix_s, n + 1)
                kv = P * (t + 1)
                for m in range(2):
                    for hd in range(HEADS):
                        ms_ = slice(64 * m, 64 * m + 64)
                        last = mm(score_view(t, m, hd), qT[ms_, hd, :], kT[ms_, hd, 0:kv], start=True, stop=True)
                last.then_inc(sc_ps, 1)
                yield 27
                pe.wait_ge(comb_ok, n + 1)
                for c in range(t + 1):
                    for hd in range(HEADS):
                        last = tr(quad(4 + c)[:, hd, :], probs[:, 0, hd, P * c:P * c + P], ident[:, :])
                last.then_inc(aT_ps, 1)
                pe.wait_ge(aT_ok, n + 1)
                for hd in range(HEADS):
                    for c in range(t + 1):
                        last = mm(quad(2)[:, hd, :], v_tok[:, c, P * hd:P * hd + P], aT[:, c, hd, :], start=c == 0, stop=c == t)
                last.then_inc(o_ps, 1)
                pe.wait_ge(o_sq_ok, n + 1)
                mm(bank[3][:, :], ones[:, :], o_sq[:, :], start=True, stop=True).then_inc(oss_ps, 1)
                yield 28
                pe.wait_ge(mix_d, n + 1)
                for c, (c0, width) in enumerate(OUT_CHUNKS):
                    w = chunk()
                    for k in range(KD):
                        last = mm(bank[c // 2][:, CW * (c % 2):CW * (c % 2) + CW], mixed[:, k, :], w[:, k, :], start=k == 0, stop=k == KD - 1)
                    chunk_used(last)

            def peer(n, layer, t):
                yield 30
                pe.wait_ge(f_h, n + 1)
                for k in range(KD):
                    last = tr(quad(2 + k // 4)[:, k % 4, :], hb[:, P * k:P * k + P], ident[:, :])
                    if k % 4 == 3:
                        last.then_inc(fT_ps, 1)
                keys = chunk().rearrange("p k (a d) -> p (k a) d", d=P)
                for i in range(4):
                    if i > 1:
                        pe.wait_ge(key_ok, 4 * n + i - 1)
                    for b in range(4):
                        last = tr(quad(4 + i % 2)[:, b, :], keys[:, 4 * i + b, :], ident[:, :])
                    if i < 3:
                        last.then_inc(key_ps, 1)
                    else:
                        chunk_used(last)
                pe.wait_ge(fT_a, n + 1)
                yield 31
                pe.wait_ge(fT_v, n + 1)
                pe.wait_ge(x_mid, n + 1)
                for c, (c0, width) in enumerate(Q_CHUNKS):
                    if c in (4, 6):
                        yield 31 + 3 * (c // 2 - 1)
                    w = chunk()
                    if c % 2 == 0 and c >= 4:
                        pe.wait_ge(pq_ok, 4 * n + c // 2 - 1)
                    for j in range(2):
                        b = 2 * (c % 2) + j
                        for k in range(KD):
                            last = mm(quad((c // 2) % 2)[:, b, :], w[:, k, P * j:P * j + P], hb_cm[:, k, :], start=k == 0, stop=k == KD - 1)
                    chunk_used(last)
                    for i in {3: (0,), 5: (1,), 7: (2, 3)}.get(c, ()):
                        if i == 0:
                            pe.wait_ge(key_ok, 4 * n + 4)
                        pe.wait_ge(pq_ok, 4 * n + i + 1)
                        for b in range(4):
                            last = mm(quad(2 + i)[:, b, :], q_cm[:, 4 * i + b, :], keys_cm[:, 4 * i + b, :], start=True, stop=True)
                        last.then_inc(ps_ps, 1)

            def gather(n, q0, q1):
                for q in range(max(q0, SLOTS), q1):
                    j, use = q % RING, USES * n + q // RING
                    if q == SLOTS:
                        if n:
                            pe.wait_ge(ffn_done, n)
                        for i in range(2):
                            mm(bank[6 + i][:, :], zeros[:, :], nothing, start=True, stop=False, skip_group_check=True)
                    if j in ON_PE:
                        pe.wait_ge(s_diag, (n * ROUNDS + q // RING - ROUNDS) * len(ON_PE) + ON_PE.index(j) + 1)
                        pe.wait_ge(s_row[j], 16 * (use + 1))
                        d = diag[:, ON_PE.index(j), :]
                        mm(bank[6][:, :], d, arena[:, j, 0:512], start=False, stop=False, skip_group_check=True)
                        mm(bank[7][:, :], d, arena[:, j, 512:1024], start=False, stop=False, skip_group_check=True)\
                            .then_inc(s_used[j], 1)
                    if q == 2 * SLOTS - 1:
                        for i in range(2):
                            last = mm(bank[6 + i][:, :], zeros[:, :], nothing, start=False, stop=True, skip_group_check=True)
                        last.then_inc(y_done, 1)

            def unit_steps(n):
                if n < UNITS:
                    yield from mixing(*units[n])
                    yield from peer(*units[n])

            for _ in unit_steps(0):
                pass
            for n, layer, t in units:
                at = 0
                for step in unit_steps(n + 1):
                    if ROWS_BY[step] > at:
                        gather(n, at, ROWS_BY[step])
                        at = ROWS_BY[step]
                gather(n, at, 2 * SLOTS)


_INS = ['x', 'positions', 'norm_mix', 'w_in', 'da_q_norm', 'da_k_norm', 'da_lambda', 'da_subln', 'ssm_lambda_re',
        'ssm_lambda_im', 'ssm_b_re', 'ssm_b_im', 'ssm_c_re', 'ssm_c_im', 'ssm_d', 'ssm_log_dt', 'ssm_w_glu',
        'ssm_b_glu', 'ssm_out_norm', 'rw_mu', 'rw_decay_up', 'rw_decay_w0', 'rw_aaa_up', 'rw_aaa_a0', 'rw_gate_up',
        'rw_k_k', 'rw_k_a', 'rw_r_k', 'rw_ln_w', 'rw_ln_b', 'w_out', 'norm_ffn', 'peer_w_q', 'peer_sub_keys',
        'peer_u', 'peer_v']


def kernel(**inputs):
    import concourse.bacc as _bacc
    from concourse.bass_utils import run_bass_kernel_spmd as _run

    nc = _bacc.Bacc("TRN2", target_bir_lowering=False, num_devices=1, dynamic_dma_scratch_size=DMA_SCRATCH)
    arrays, args = {}, {}
    for name in _INS:
        a = np.ascontiguousarray(inputs[name])
        arrays[f"in_{name}_dram"] = a
        args[name] = nc.dram_tensor(f"in_{name}_dram", a.shape, mybir.dt.from_np(a.dtype), kind="ExternalInput").ap()
    out = nc.dram_tensor("out_0_dram", (1, SEQ, D_MODEL), F32, kind="ExternalOutput").ap()
    build_program(nc, args, out)
    r = _run(nc, [arrays], core_ids=[0])
    return r.results[0]["out_0_dram"]
```
